# Optimizing a Trainium2 kernel written in Bass

```python
import math
import jax, jax.numpy as jnp
from jax import lax
import numpy as np

D_MODEL = 1024
BATCH = 1
SEQ = 512
DEPTH = 1
DEC_BATCH = 1
DEC_SEQ = 512
PAST_LEN = 128

D_POOL = 512
POOL_WINDOWS = (2, 4, 8, 16)
N_POOL_GROUPS = len(POOL_WINDOWS)
POOL_GROUP = D_POOL // N_POOL_GROUPS
D_HYENA = 512
HYENA_ORDER = 2
SHORT_CONV = 3
FILTER_EMB = 33
FILTER_HIDDEN = 64
DECAY_TARGET = 1e-2
FAST_DECAY_PCT = 0.3
SLOW_DECAY_PCT = 1.5
N_BRANCH = 2
D_IN = D_POOL + (HYENA_ORDER + 1) * D_HYENA + N_BRANCH * D_MODEL
PEER_HEADS = 8
PEER_NKEYS = 128
PEER_EXPERTS = PEER_NKEYS * PEER_NKEYS
PEER_DQ = 256
PEER_DHALF = PEER_DQ // 2
PEER_TOPK = 16
TOKEN_BLOCK = 128
EPS = 1e-6

kernel_name = "pool_hyena_peer_gated_encoder"

def rmsnorm(x, g):
    xf = x.astype(jnp.float32)
    y = xf * lax.rsqrt(jnp.mean(xf * xf, axis=-1, keepdims=True) + EPS)
    return (y * g.astype(jnp.float32)).astype(x.dtype)

def multiscale_pool(a, pool_w, pool_scale):
    B, L, _ = a.shape
    af = a.astype(jnp.float32).reshape(B, L, N_POOL_GROUPS, POOL_GROUP)
    t = jnp.arange(L)
    outs = []
    for g, w in enumerate(POOL_WINDOWS):
        half = w // 2
        xg = af[:, :, g]
        xp = jnp.pad(xg, ((0, 0), (half + 1, half), (0, 0)))
        c = jnp.cumsum(xp, axis=1)
        win = c[:, w:w + L] - c[:, 0:L]
        cnt = (jnp.minimum(t + half, L) - jnp.maximum(t - half, 0)).astype(jnp.float32)
        outs.append(win / cnt[None, :, None] - xg)
    pooled = jnp.stack(outs, axis=2)
    mixed = jnp.einsum('blgc,gcd->blgd', pooled, pool_w.astype(jnp.float32))
    return (mixed.reshape(B, L, D_POOL) * pool_scale.astype(jnp.float32)).astype(a.dtype)

def short_conv(u, w, b):
    L = u.shape[1]
    up = jnp.pad(u, ((0, 0), (1, 1), (0, 0)))
    return up[:, 0:L] * w[0] + up[:, 1:L + 1] * w[1] + up[:, 2:L + 2] * w[2] + b

def hyena_filters(L, w1, b1, f1, w2, b2, f2, w3):
    f32 = jnp.float32
    t = jnp.linspace(0.0, 1.0, L, dtype=f32)[:, None]
    bands = (FILTER_EMB - 1) // 2
    wpos = 2.0 * math.pi * jnp.arange(L, dtype=f32)[:, None] / L
    freqs = jnp.linspace(1e-4, bands - 1, bands, dtype=f32)[None, :]
    z = jnp.concatenate([t, jnp.cos(freqs * wpos), -jnp.sin(freqs * wpos)], axis=-1)
    h = jnp.sin(f1.astype(f32) * (z @ w1.astype(f32) + b1.astype(f32)))
    h = jnp.sin(f2.astype(f32) * (h @ w2.astype(f32) + b2.astype(f32)))
    h = h @ w3.astype(f32)
    max_decay = math.log(DECAY_TARGET) / FAST_DECAY_PCT
    min_decay = math.log(DECAY_TARGET) / SLOW_DECAY_PCT
    deltas = jnp.linspace(min_decay, max_decay, D_HYENA, dtype=f32)
    decay = jnp.exp(-t * jnp.abs(deltas)[None, :])
    h = h.reshape(L, 2, D_HYENA) * decay[:, None, :]
    return h[:, 0], h[:, 1]

def bidirectional_fftconv(z, kf, kb):
    L = z.shape[1]
    k = jnp.concatenate([kf.at[0].add(kb[0]), jnp.zeros((1, D_HYENA), jnp.float32), kb[1:][::-1]], axis=0)
    k_f = jnp.fft.rfft(k, axis=0)
    z_f = jnp.fft.rfft(z, n=2 * L, axis=1)
    return jnp.fft.irfft(z_f * k_f[None], n=2 * L, axis=1)[:, :L]

def hyena_mixer(u, conv_w, conv_b, w1, b1, f1, w2, b2, f2, w3, bias):
    L = u.shape[1]
    uc = short_conv(u, conv_w, conv_b)
    x0, x1, v = jnp.split(uc, 3, axis=-1)
    z = (v * x1).astype(jnp.float32)
    kf, kb = hyena_filters(L, w1, b1, f1, w2, b2, f2, w3)
    y = bidirectional_fftconv(z, kf, kb) + z * bias.astype(jnp.float32)
    return (y * x0.astype(jnp.float32)).astype(u.dtype)

def peer_block(xb, wq, keys, u_tab, v_tab):
    T = xb.shape[0]
    q = (xb @ wq).reshape(T, PEER_HEADS, 2, PEER_DHALF)
    s = jnp.einsum('thpc,hpkc->thpk', q, keys).astype(jnp.float32)
    sv, si = lax.top_k(s, PEER_TOPK)
    cand = (sv[:, :, 0, :, None] + sv[:, :, 1, None, :]).reshape(T, PEER_HEADS, PEER_TOPK * PEER_TOPK)
    cand_idx = (si[:, :, 0, :, None] * PEER_NKEYS + si[:, :, 1, None, :]).reshape(T, PEER_HEADS, PEER_TOPK * PEER_TOPK)
    best, pos = lax.top_k(cand, PEER_TOPK)
    idx = jnp.take_along_axis(cand_idx, pos, axis=-1).reshape(T, PEER_HEADS * PEER_TOPK)
    gate = jax.nn.softmax(best, axis=-1).reshape(T, PEER_HEADS * PEER_TOPK)
    u_g = jnp.take(u_tab, idx, axis=0)
    v_g = jnp.take(v_tab, idx, axis=0)
    act = jax.nn.gelu(jnp.einsum('ted,td->te', u_g, xb).astype(jnp.float32)) * gate
    return jnp.einsum('te,ted->td', act.astype(xb.dtype), v_g)

def peer(x, wq, keys, u_tab, v_tab):
    B, L, D = x.shape
    blocks = x.reshape(B * (L // TOKEN_BLOCK), TOKEN_BLOCK, D)
    out = lax.map(lambda blk: peer_block(blk, wq, keys, u_tab, v_tab), blocks)
    return out.reshape(B, L, D)

def encoder_layer(x, norm1_g, w_in, pool_w, pool_scale, conv_w, conv_b, filt_w1, filt_b1, filt_f1,
                  filt_w2, filt_b2, filt_f2, filt_w3, hyena_bias, w_pool_out, w_hyena_out, w_o,
                  norm2_g, peer_wq, peer_keys, peer_u, peer_v):
    xn = rmsnorm(x, norm1_g)
    proj = xn @ w_in
    a, hy, gates = jnp.split(proj, [D_POOL, D_POOL + (HYENA_ORDER + 1) * D_HYENA], axis=-1)
    gate_a, gate_b = jnp.split(gates, N_BRANCH, axis=-1)
    ya = multiscale_pool(a, pool_w, pool_scale) @ w_pool_out
    yb = hyena_mixer(hy, conv_w, conv_b, filt_w1, filt_b1, filt_f1, filt_w2, filt_b2, filt_f2,
                     filt_w3, hyena_bias) @ w_hyena_out
    mixed = jax.nn.sigmoid(gate_a) * ya + jax.nn.sigmoid(gate_b) * yb
    h = x + mixed @ w_o
    return h + peer(rmsnorm(h, norm2_g), peer_wq, peer_keys, peer_u, peer_v)

def setup_inputs(seed: int = 0) -> dict:
    key = jax.random.key(seed)
    ks = jax.random.split(key, 26)
    f32 = jnp.float32
    nrm = lambda k, shape, scale: jax.random.normal(k, shape, f32) * scale
    L_ = DEPTH
    return {
        "x_prompt": nrm(ks[0], (BATCH, SEQ, D_MODEL), 1.0),
        "x_sample": nrm(ks[1], (DEC_BATCH, DEC_SEQ, D_MODEL), 1.0),
        "norm1_g": 1.0 + nrm(ks[2], (L_, D_MODEL), 0.05),
        "w_in": nrm(ks[3], (L_, D_MODEL, D_IN), D_MODEL ** -0.5),
        "pool_w": nrm(ks[4], (L_, N_POOL_GROUPS, POOL_GROUP, POOL_GROUP), POOL_GROUP ** -0.5),
        "pool_scale": 1.0 + nrm(ks[5], (L_, D_POOL), 0.1),
        "conv_w": nrm(ks[6], (L_, SHORT_CONV, (HYENA_ORDER + 1) * D_HYENA), SHORT_CONV ** -0.5),
        "conv_b": nrm(ks[7], (L_, (HYENA_ORDER + 1) * D_HYENA), 0.01),
        "filt_w1": nrm(ks[8], (L_, FILTER_EMB, FILTER_HIDDEN), FILTER_EMB ** -0.5),
        "filt_b1": nrm(ks[9], (L_, FILTER_HIDDEN), 0.1),
        "filt_f1": 1.0 + nrm(ks[10], (L_, FILTER_HIDDEN), 0.1),
        "filt_w2": nrm(ks[11], (L_, FILTER_HIDDEN, FILTER_HIDDEN), FILTER_HIDDEN ** -0.5),
        "filt_b2": nrm(ks[12], (L_, FILTER_HIDDEN), 0.1),
        "filt_f2": 1.0 + nrm(ks[13], (L_, FILTER_HIDDEN), 0.1),
        "filt_w3": nrm(ks[14], (L_, FILTER_HIDDEN, 2 * D_HYENA), 0.04 * FILTER_HIDDEN ** -0.5),
        "hyena_bias": nrm(ks[15], (L_, D_HYENA), 1.0),
        "w_pool_out": nrm(ks[16], (L_, D_POOL, D_MODEL), D_POOL ** -0.5),
        "w_hyena_out": nrm(ks[17], (L_, D_HYENA, D_MODEL), D_HYENA ** -0.5),
        "w_o": nrm(ks[18], (L_, D_MODEL, D_MODEL), D_MODEL ** -0.5),
        "norm2_g": 1.0 + nrm(ks[19], (L_, D_MODEL), 0.05),
        "peer_wq": nrm(ks[20], (L_, D_MODEL, PEER_HEADS * PEER_DQ), D_MODEL ** -0.5),
        "peer_keys": nrm(ks[21], (L_, PEER_HEADS, 2, PEER_NKEYS, PEER_DHALF), PEER_DHALF ** -0.5),
        "peer_u": nrm(ks[22], (L_, PEER_EXPERTS, D_MODEL), D_MODEL ** -0.5),
        "peer_v": nrm(ks[23], (L_, PEER_EXPERTS, D_MODEL), PEER_TOPK ** -0.5),
        "normf_g": 1.0 + nrm(ks[24], (D_MODEL,), 0.05),
    }

def reference(x_prompt, x_sample, norm1_g, w_in, pool_w, pool_scale, conv_w, conv_b, filt_w1, filt_b1,
              filt_f1, filt_w2, filt_b2, filt_f2, filt_w3, hyena_bias, w_pool_out, w_hyena_out, w_o,
              norm2_g, peer_wq, peer_keys, peer_u, peer_v, normf_g):
    def trunk(x):
        for l in range(DEPTH):
            x = encoder_layer(x, norm1_g[l], w_in[l], pool_w[l], pool_scale[l], conv_w[l], conv_b[l],
                              filt_w1[l], filt_b1[l], filt_f1[l], filt_w2[l], filt_b2[l], filt_f2[l],
                              filt_w3[l], hyena_bias[l], w_pool_out[l], w_hyena_out[l], w_o[l],
                              norm2_g[l], peer_wq[l], peer_keys[l], peer_u[l], peer_v[l])
        return rmsnorm(x, normf_g)

    y_prompt = trunk(x_prompt)
    y_sample = trunk(x_sample)
    return (y_prompt, y_sample)


_drawn_inputs = setup_inputs


def setup_inputs(seed=0):
    import zlib

    import numpy as np

    out = dict(_drawn_inputs(seed))
    spreads = {}
    factors = {'conv_b': 4.427, 'filt_b1': 3.514, 'filt_f1': 5.539, 'filt_b2': 3.551, 'filt_f2': 6.09}
    for name, (base, spread) in spreads.items():
        noise = np.random.default_rng([zlib.crc32(name.encode()), seed]).standard_normal(out[name].shape)
        drawn = base * np.exp(spread * noise) if base else spread * noise
        out[name] = __import__('jax').numpy.asarray(drawn.astype(out[name].dtype))
    for name, factor in factors.items():
        out[name] = (out[name] * factor).astype(out[name].dtype)
    return out
```

```python
from contextlib import ExitStack

import concourse.bass as bass
import numpy as np
from concourse import mybir

F32 = mybir.dt.float32
F32R = mybir.dt.float32r
U32 = mybir.dt.uint32
ALU = mybir.AluOpType
ACT = mybir.ActivationFunctionType
X = mybir.AxisListType.X

P = 128
D = 1024
KD = D // P
NSEQ = 2
L = 512
T = NSEQ * L
TT = T // P
LT = L // P
C = 512
CT = C // P
WINDOWS = (2, 4, 8, 16)
PAD = 8
N_FFT = 2 * L
H = 8
NK = 128
TOPK = 16
HID = 64
FEMB = 33
EPS = 1e-6
LOWEST = -3.0e38
A_T, X0_T, X1_T, V_T, GA_T, GB_T = 0, 4, 8, 12, 16, 24
TWO_PI = (6.28125, 1.9353071693331003e-3, 1.0253131677018246e-11)
ROUND = 12582912.0
ONE = 1


class Steps:

    def __init__(self, eng, sem, base=0, start=0):
        self.eng, self.sem, self.base, self.start, self.n = eng, sem, base, start, 0

    def did(self, ins):
        ins.then_inc(self.sem, 1)
        self.n += 1
        return ins

    def settle(self):
        self.eng.wait_ge(self.sem, self.start + self.base + self.n)


def f32(ap):
    return ap.bitcast(F32)


class Mem:

    def __init__(self, nc, ctx, side="left"):
        self.nc, self.ctx, self.side, self.sems, self.held = nc, ctx, side, [], []

    def sb(self, name, shape, dt=F32):
        return self.ctx.enter_context(self.nc.sbuf_tensor(name, shape, dt, side=self.side))

    def ps(self, name, shape):
        return self.ctx.enter_context(self.nc.psum_tensor(name, shape, F32))

    def sem(self, name):
        self.held.append(self.nc.semaphore(name))
        self.sems.append(self.held[-1].__enter__())
        return self.sems[-1]

    def release(self):
        with self.nc.Block() as block:
            @block.sync
            def _(sp):
                for sem in self.sems:
                    sp.sem_clear(sem)
        while self.held:
            self.held.pop().__exit__(None, None, None)

    def start_at_one(self, sp):
        for sem in self.sems:
            sp.sem_inc(sem, ONE)


def products(pe, out, w_hi, w_lo, m_hi, m_lo, first, last):
    pe.matmul(out, w_lo, m_hi, start=first, stop=False)
    pe.matmul(out, w_hi, m_lo, start=False, stop=False)
    return pe.matmul(out, w_hi, m_hi, start=False, stop=last)


def filters(nc, dram, K):
    with ExitStack() as ctx:
        m = Mem(nc, ctx)
        ctx.callback(m.release)
        dft = m.sb("dft", [P, LT, N_FFT])
        pos = m.sb("filt_pos", [FEMB, L])
        w1 = m.sb("filt_w1", [FEMB, HID])
        w2 = m.sb("filt_w2", [HID, HID])
        w3 = m.sb("filt_w3", [HID, 2 * C])
        vec = m.sb("filt_vec", [HID, 4])
        decay = m.sb("decay", [P, LT, C])
        h1 = m.sb("h1", [HID, L])
        turns = m.sb("turns", [HID, L])
        h2 = m.sb("h2", [HID, L])
        fwd = m.sb("fwd", [P, LT, C])
        bwd = m.sb("bwd", [P, LT, C])
        even = m.sb("even", [P, LT, C])
        even_hi, even_lo = m.sb("even_hi", [P, LT, C], F32R), m.sb("even_lo", [P, LT, C], F32R)
        odd_hi, odd_lo = m.sb("odd_hi", [P, LT, C], F32R), m.sb("odd_lo", [P, LT, C], F32R)
        net_ps = m.ps("net_ps", [HID, L])
        taps_ps = [m.ps(f"taps_ps{b}", [P, C]) for b in range(2)]
        spec_ps = [m.ps(f"spec_ps{b}", [P, C]) for b in range(2)]
        small_in, dft_in, decay_in = m.sem("small_in"), m.sem("dft_in"), m.sem("decay_in")
        net_done, sin_done = m.sem("net_done"), m.sem("sin_done")
        arg_done, taps_done, taps_read = m.sem("arg_done"), m.sem("taps_done"), m.sem("taps_read")
        hi_done, lo_done = m.sem("fhi_done"), m.sem("flo_done")
        spec_done, spec_read = m.sem("spec_done"), m.sem("spec_read")
        vsteps = m.sem("f_vsteps")
        block = ctx.enter_context(nc.Block())

        @block.sync
        def _(sp):
            for dst, name in ((pos, "filt_pos"), (w1, "filt_w1"), (w2, "filt_w2"), (w3, "filt_w3"), (vec, "filt_vec")):
                sp.dma_start(dst[:], dram[name]).then_inc(small_in, 16)
            sp.dma_start(decay[:], dram["decay"]).then_inc(decay_in, 16)
            sp.dma_start(dft[:], dram["dft"]).then_inc(dft_in, 16)

        @block.tensor
        def _(pe):
            pe.wait_ge(small_in, 5 * 16)
            pe.matmul(net_ps[:], w1[:], pos[:], start=True, stop=True).then_inc(net_done, 1)
            pe.wait_ge(sin_done, 1)
            pe.matmul(net_ps[:], w2[:], h1[:], start=True, stop=True).then_inc(net_done, 1)
            pe.wait_ge(sin_done, 2)
            for n in range(2 * LT):
                lt, half = n // 2, n % 2
                if n >= 2:
                    pe.wait_ge(taps_read, n - 1)
                pe.matmul(taps_ps[half][:], h2[:, lt * P:(lt + 1) * P], w3[:, half * C:(half + 1) * C],
                          start=True, stop=True).then_inc(taps_done, 1)
            pe.wait_ge(lo_done, 3)
            for n, (col, hi, lo) in enumerate(
                    [(kt, even_hi, even_lo) for kt in range(4)] + [(kt, odd_hi, odd_lo) for kt in range(4, 8)]
                    + [(4, even_hi, even_lo)]):
                if n >= 2:
                    pe.wait_ge(spec_read, n - 1)
                for c in range(LT):
                    last = products(pe, spec_ps[n % 2][:], K["dft_hi"][:, c, col * P:(col + 1) * P],
                                    K["dft_lo"][:, c, col * P:(col + 1) * P], hi[:, c], lo[:, c], c == 0, c == LT - 1)
                last.then_inc(spec_done, 1)

        @block.scalar
        def _(act):
            act.wait_ge(dft_in, 16)
            act.activation(K["dft_hi"][:], dft[:], ACT.Copy).then_inc(hi_done, 1)
            act.wait_ge(arg_done, 1)
            act.activation(h1[:], turns[:], ACT.Sin).then_inc(sin_done, 1)
            act.wait_ge(arg_done, 2)
            act.activation(h2[:], turns[:], ACT.Sin).then_inc(sin_done, 1)
            act.wait_ge(taps_read, 2 * LT + 1)
            act.activation(even_hi[:], even[:], ACT.Copy).then_inc(hi_done, 1)
            act.wait_ge(taps_read, 2 * LT + 2)
            act.activation(odd_hi[:], fwd[:], ACT.Copy).then_inc(hi_done, 1)

        @block.vector
        def _(dve):
            s = Steps(dve, vsteps)
            dve.wait_ge(small_in, 5 * 16)
            for layer in range(2):
                b, f = vec[:, 2 * layer:2 * layer + 1], vec[:, 2 * layer + 1:2 * layer + 2]
                arg = h2 if layer == 0 else h1
                dve.wait_ge(net_done, layer + 1)
                s.did(dve.tensor_scalar(arg[:], net_ps[:], b, f, ALU.add, ALU.mult))
                s.settle()
                if layer == 1:
                    dve.wait_ge(sin_done, 1)
                s.did(dve.tensor_scalar(turns[:], arg[:], 1.0 / (2 * np.pi), ROUND, ALU.mult, ALU.add))
                s.settle()
                s.did(dve.tensor_scalar(turns[:], turns[:], ROUND, None, ALU.subtract))
                s.settle()
                for part in TWO_PI:
                    s.did(dve.scalar_tensor_tensor(out=arg[:], in0=turns[:], scalar=-part, in1=arg[:],
                                                   op0=ALU.mult, op1=ALU.add))
                    s.settle()
                dve.tensor_scalar(turns[:], arg[:], 3.1415925, -3.1415925, ALU.min, ALU.max).then_inc(arg_done, 1)
            dve.wait_ge(decay_in, 16)
            for n in range(2 * LT):
                dve.wait_ge(taps_done, n + 1)
                dve.tensor_tensor((fwd, bwd)[n % 2][:, n // 2], taps_ps[n % 2][:], decay[:, n // 2],
                                  ALU.mult).then_inc(taps_read, 1)
            dve.wait_ge(taps_read, 2 * LT)
            dve.tensor_tensor(even[:], fwd[:], bwd[:], ALU.add).then_inc(taps_read, 1)
            dve.wait_ge(taps_read, 2 * LT + 1)
            dve.tensor_tensor(fwd[:], fwd[:], bwd[:], ALU.subtract).then_inc(taps_read, 1)
            dve.wait_ge(hi_done, 1)
            dve.wait_ge(dft_in, 16)
            dve.tensor_tensor(K["dft_lo"][:], dft[:], f32(K["dft_hi"][:]), ALU.subtract).then_inc(lo_done, 1)
            dve.wait_ge(hi_done, 2)
            dve.tensor_tensor(even_lo[:], even[:], f32(even_hi[:]), ALU.subtract).then_inc(lo_done, 1)
            dve.wait_ge(hi_done, 3)
            dve.tensor_tensor(odd_lo[:], fwd[:], f32(odd_hi[:]), ALU.subtract).then_inc(lo_done, 1)
            for n in range(9):
                dve.wait_ge(spec_done, n + 1)
                if n < 4:
                    dve.tensor_copy(K["k_re"][:, n], spec_ps[n % 2][:]).then_inc(spec_read, 1)
                elif n < 8:
                    dve.tensor_copy(K["k_im"][:, n - 4], spec_ps[n % 2][:]).then_inc(spec_read, 1)
                else:
                    dve.wait_ge(spec_read, 8)
                    s.did(dve.tensor_copy(K["k_re0"][:], K["k_re"][:, 0]))
                    s.settle()
                    dve.tensor_copy(K["k_re0"][0:1, :], spec_ps[n % 2][0:1, :]).then_inc(spec_read, 1)
                    dve.memset(K["k_im"][0:1, 0], 0.0).then_inc(spec_read, 1)


def norm_transpose(nc, dram, tag, load, src, gain, keep, x_hi, x_lo):
    with ExitStack() as ctx:
        m = Mem(nc, ctx)
        ctx.callback(m.release)
        gain_sb = m.sb(f"{tag}_gain", [P, D])
        ident = m.sb(f"{tag}_ident", [P, P])
        normed = [m.sb(f"{tag}_normed{b}", [P, D]) for b in range(2)]
        sq = m.sb(f"{tag}_sq", [P, D])
        ss, rstd = m.sb(f"{tag}_ss", [P, TT]), m.sb(f"{tag}_rstd", [P, TT])
        tp = [m.ps(f"{tag}_tp{b}", [P, KD, P]) for b in range(2)]
        src_in = [m.sem(f"{tag}_src_in{s}") for s in range(NSEQ)]
        const_in, kept = m.sem(f"{tag}_const_in"), m.sem(f"{tag}_kept")
        squared, ms_done, root, inv = (m.sem(f"{tag}_{n}") for n in ("squared", "ms_done", "root", "inv"))
        normed_done, turned = m.sem(f"{tag}_normed_done"), m.sem(f"{tag}_turned")
        hi_done, lo_done = m.sem(f"{tag}_hi_done"), m.sem(f"{tag}_lo_done")
        block = ctx.enter_context(nc.Block())

        @block.sync
        def _(sp):
            m.start_at_one(sp)
            sp.dma_start(ident[:], dram["ident"]).then_inc(const_in, 16)
            sp.dma_start(gain_sb[:], dram[gain].broadcast_to([P, D])).then_inc(const_in, 16)
            if load is not None:
                for s in range(NSEQ):
                    sp.dma_start(src[:, s * LT:(s + 1) * LT], load[s]).then_inc(src_in[s], 16)
            if keep is not None:
                sp.dma_start(keep, src[:]).then_inc(kept, 16)
                sp.wait_ge(kept, ONE + 16)

        @block.scalar
        def _(act):
            for tt in range(TT):
                if load is not None:
                    act.wait_ge(src_in[tt // LT], ONE + 16)
                if tt:
                    act.wait_ge(squared, ONE + tt)
                act.activation(sq[:], src[:, tt], ACT.Square, accum_out=ss[:, tt:tt + 1]).then_inc(squared, 1)
            act.wait_ge(ms_done, ONE + 1)
            act.activation(rstd[:], ss[:], ACT.Sqrt).then_inc(root, 1)
            with act.Fori(0, TT // 2) as i:
                for b in range(2):
                    act.wait_ge(turned, ONE + 2 * i + b + 1)
                    act.activation(x_hi[:, :, bass.ts(2 * i + b, P)], tp[b][:], ACT.Copy).then_inc(hi_done, 1)

        @block.vector
        def _(dve):
            dve.wait_ge(squared, ONE + TT)
            dve.tensor_scalar(ss[:], ss[:], 1.0 / D, EPS, ALU.mult, ALU.add).then_inc(ms_done, 1)
            dve.wait_ge(root, ONE + 1)
            dve.reciprocal(rstd[:], rstd[:]).then_inc(inv, 1)
            dve.wait_ge(inv, ONE + 1)
            dve.wait_ge(const_in, ONE + 32)
            if load is not None:
                for s in range(NSEQ):
                    dve.wait_ge(src_in[s], ONE + 16)

            with dve.Fori(0, TT // 2) as i:
                for b in range(2):
                    tt = 2 * i + b
                    dve.wait_ge(turned, ONE + tt)
                    dve.scalar_tensor_tensor(out=normed[b][:], in0=src[:, tt], scalar=rstd[:, bass.ds(tt, 1)],
                                             in1=gain_sb[:], op0=ALU.mult, op1=ALU.mult).then_inc(normed_done, 1)
                    dve.wait_ge(hi_done, ONE + tt + 1)
                    dve.tensor_tensor(x_lo[:, :, bass.ts(tt, P)], tp[b][:], f32(x_hi[:, :, bass.ts(tt, P)]),
                                      ALU.subtract).then_inc(lo_done, 1)

        @block.tensor
        def _(pe):
            pe.wait_ge(const_in, ONE + 32)
            with pe.Fori(0, TT // 2) as i:
                for b in range(2):
                    pe.wait_ge(normed_done, ONE + 2 * i + b + 1)
                    if b == 0:
                        pe.wait_ge(lo_done, ONE + 2 * i)
                    for k in range(KD):
                        t = pe.transpose(tp[b][:, k], normed[b][:, k * P:(k + 1) * P], ident[:])
                    t.then_inc(turned, 1)


class Stream:

    def __init__(self, m, tag, slots):
        self.slots = slots
        self.raw = [m.sb(f"{tag}_raw{b}", [P, D]) for b in range(slots)]
        self.hi = [m.sb(f"{tag}_hi{b}", [P, D], F32R) for b in range(slots)]
        self.lo = [m.sb(f"{tag}_lo{b}", [P, D], F32R) for b in range(slots)]
        self.landed = [m.sem(f"{tag}_landed{b}") for b in range(slots)]
        self.hi_done, self.lo_done, self.used = (m.sem(f"{tag}_{n}") for n in ("hi_done", "lo_done", "used"))


def split_first(act, st):
    act.wait_ge(st.landed[0], ONE + 16)
    act.activation(st.hi[0][:], st.raw[0][:], ACT.Copy).then_inc(st.hi_done, 1)


def split_next(act, st, i, b):
    n = 1 - b
    act.wait_ge(st.landed[n], ONE + 16 * (i + b) + 16)
    if b:
        act.wait_ge(st.used, ONE + 2 * i + 1)
    else:
        act.wait_ge(st.used, ONE + 2 * i)
    act.activation(st.hi[n][:], st.raw[n][:], ACT.Copy).then_inc(st.hi_done, 1)


def project_conv(nc, K, b, ps, uc, conv_col, dve, s):
    w = K["conv_w"]
    s.did(dve.scalar_tensor_tensor(out=uc[:, :, 1:L], in0=ps[:, :, 0:L - 1], scalar=w[:, 0, bass.ds(conv_col, 1)],
                                   in1=uc[:, :, 1:L], op0=ALU.mult, op1=ALU.add))
    s.settle()
    return dve.scalar_tensor_tensor(out=uc[:, :, 0:L - 1], in0=ps[:, :, 1:L], scalar=w[:, 2, bass.ds(conv_col, 1)],
                                    in1=uc[:, :, 0:L - 1], op0=ALU.mult, op1=ALU.add)


def gate_product(nc, dram, K, x_hi, x_lo, z_t):
    with ExitStack() as ctx:
        m = Mem(nc, ctx)
        st = Stream(m, "zw", 2)
        uc = [m.sb(f"z_uc{b}", [P, NSEQ, L]) for b in range(2)]
        ps = [m.ps(f"z_ps{b}", [P, NSEQ, L]) for b in range(2)]
        conv_in, mid, read, zdone, vs = (m.sem(f"z_{n}") for n in ("conv_in", "mid", "read", "done", "vs"))
        block = ctx.enter_context(nc.Block())

        @block.sync
        def _(sp):
            m.start_at_one(sp)
            sp.dma_start(K["conv_w"][:], dram["conv_w"]).then_inc(conv_in, 16)
            sp.dma_start(K["conv_b"][:], dram["conv_b"]).then_inc(conv_in, 16)
            with sp.Fori(0, CT) as i:
                for b in range(2):
                    sp.wait_ge(st.lo_done, ONE + 2 * i)
                    sp.dma_start(st.raw[b][:], dram["w_in"][bass.ds(i + (X1_T, V_T)[b], 1)]).then_inc(st.landed[b], 16)

        @block.gpsimd
        def _(pool):
            with pool.Fori(0, CT) as i:
                for b in range(2):
                    pool.wait_ge(st.hi_done, ONE + 2 * i + b + 1)
                    pool.tensor_tensor(st.lo[b][:], st.raw[b][:], f32(st.hi[b][:]), ALU.subtract).then_inc(st.lo_done, 1)

        @block.tensor
        def _(pe):
            with pe.Fori(0, CT) as i:
                for b in range(2):
                    pe.wait_ge(st.lo_done, ONE + 2 * i + b + 1)
                    pe.wait_ge(read, ONE + 2 * i)
                    for k in range(KD):
                        c = slice(k * P, (k + 1) * P)
                        for s in range(NSEQ):
                            t = slice(s * L, (s + 1) * L)
                            last = products(pe, ps[b][:, s], st.hi[b][:, c], st.lo[b][:, c], x_hi[:, k, t],
                                            x_lo[:, k, t], k == 0, k == KD - 1)
                    last.then_inc(st.used, 1)

        @block.scalar
        def _(act):
            act.wait_ge(conv_in, ONE + 32)

            def turn(i, b, ahead):
                if ahead:
                    split_next(act, st, i, b)
                act.wait_ge(st.used, ONE + 2 * i + b + 1)
                act.wait_ge(zdone, ONE + i)
                col = i + (X1_T, V_T)[b] - X0_T
                act.activation(uc[b][:], ps[b][:], ACT.Identity, bias=K["conv_b"][:, bass.ds(col, 1)],
                               scale=K["conv_w"][:, 1, bass.ds(col, 1)]).then_inc(mid, 1)

            split_first(act, st)
            with act.Fori(0, CT - 1) as i:
                for b in range(2):
                    turn(i, b, True)
            turn(CT - 1, 0, True)
            turn(CT - 1, 1, False)

        @block.vector
        def _(dve):
            with dve.Fori(0, CT) as i:
                s = Steps(dve, vs, 2 * i, ONE)
                for b in range(2):
                    dve.wait_ge(mid, ONE + 2 * i + b + 1)
                    project_conv(nc, K, b, ps[b], uc[b], i + (X1_T, V_T)[b] - X0_T, dve, s).then_inc(read, 1)
                dve.wait_ge(read, ONE + 2 * i + 2)
                dve.tensor_tensor(z_t[:, i], uc[0][:].rearrange("p s t -> p (s t)"),
                                  uc[1][:].rearrange("p s t -> p (s t)"), ALU.mult).then_inc(zdone, 1)


def forward_dft(nc, dram, K, z_t, y_spec):
    with ExitStack() as ctx:
        m = Mem(nc, ctx)
        ident = m.sb("fd_ident", [P, P])
        z_hi, z_lo = m.sb("z_hi", [P, TT, C], F32R), m.sb("z_lo", [P, TT, C], F32R)
        prod = [m.sb(f"fd_prod{n}", [P, C]) for n in range(4)]
        tp = [m.ps(f"fd_tp{b}", [P, CT, P]) for b in range(2)]
        re = [m.ps(f"fd_re{b}", [P, C]) for b in range(2)]
        im = [m.ps(f"fd_im{b}", [P, C]) for b in range(2)]
        ident_in, turned, hi_done, lo_done = (m.sem(f"fd_{n}") for n in ("ident_in", "turned", "hi", "lo"))
        spec, mult, summed = (m.sem(f"fd_{n}") for n in ("spec", "mult", "summed"))
        block = ctx.enter_context(nc.Block())
        jobs = [(s, kt) for s in range(NSEQ) for kt in range(4)]

        @block.sync
        def _(sp):
            m.start_at_one(sp)
            sp.dma_start(ident[:], dram["ident"]).then_inc(ident_in, 16)

        @block.tensor
        def _(pe):
            pe.wait_ge(ident_in, ONE + 16)
            for tt in range(TT):
                if tt >= 2:
                    pe.wait_ge(lo_done, ONE + tt - 1)
                for c in range(CT):
                    t = pe.transpose(tp[tt % 2][:, c], z_t[:, c, tt * P:(tt + 1) * P], ident[:])
                t.then_inc(turned, 1)
            for n, (s, kt) in enumerate(jobs):
                pe.wait_ge(lo_done, ONE + LT * (s + 1))
                if n >= 2:
                    pe.wait_ge(mult, ONE + n - 1)
                for half, out in ((0, re), (1, im)):
                    col = slice((4 * half + kt) * P, (4 * half + kt + 1) * P)
                    for c in range(LT):
                        last = products(pe, out[n % 2][:], K["dft_hi"][:, c, col], K["dft_lo"][:, c, col],
                                        z_hi[:, s * LT + c], z_lo[:, s * LT + c], c == 0, c == LT - 1)
                last.then_inc(spec, 1)

        @block.scalar
        def _(act):
            for tt in range(TT):
                act.wait_ge(turned, ONE + tt + 1)
                act.activation(z_hi[:, tt], tp[tt % 2][:], ACT.Copy).then_inc(hi_done, 1)

        @block.vector
        def _(dve):
            for tt in range(TT):
                dve.wait_ge(hi_done, ONE + tt + 1)
                dve.tensor_tensor(z_lo[:, tt], tp[tt % 2][:], f32(z_hi[:, tt]), ALU.subtract).then_inc(lo_done, 1)
            for n, (s, kt) in enumerate(jobs):
                k_re, k_im = K["k_re"][:, kt], K["k_im"][:, kt]
                k_re_im = K["k_re0"][:] if kt == 0 else k_re
                dve.wait_ge(spec, ONE + n + 1)
                if n:
                    dve.wait_ge(summed, ONE + 2 * n)
                dve.tensor_tensor(prod[0][:], re[n % 2][:], k_re, ALU.mult)
                dve.tensor_tensor(prod[1][:], im[n % 2][:], k_im, ALU.mult)
                dve.tensor_tensor(prod[2][:], re[n % 2][:], k_im, ALU.mult)
                dve.tensor_tensor(prod[3][:], im[n % 2][:], k_re_im, ALU.mult).then_inc(mult, 1)

        @block.gpsimd
        def _(pool):
            for n, (s, kt) in enumerate(jobs):
                pool.wait_ge(mult, ONE + n + 1)
                pool.tensor_tensor(y_spec[:, kt, s], prod[0][:], prod[1][:], ALU.subtract).then_inc(summed, 1)
                pool.tensor_tensor(y_spec[:, 4 + kt, s], prod[2][:], prod[3][:], ALU.add).then_inc(summed, 1)


def inverse_dft(nc, dram, y_spec, z_t):
    with ExitStack() as ctx:
        m = Mem(nc, ctx)
        idft = m.sb("idft", [P, 8, L])
        g_hi, g_lo = m.sb("idft_hi", [P, 8, L], F32R), m.sb("idft_lo", [P, 8, L], F32R)
        y_hi, y_lo = m.sb("ys_hi", [P, 8, C], F32R), m.sb("ys_lo", [P, 8, C], F32R)
        bias = m.sb("hy_bias", [P, CT])
        ps = [m.ps(f"id_ps{b}", [P, L]) for b in range(2)]
        idft_in, bias_in, hi_done, lo_done, inv, read = (
            m.sem(f"id_{n}") for n in ("in", "bias_in", "hi", "lo", "inv", "read"))
        block = ctx.enter_context(nc.Block())

        @block.sync
        def _(sp):
            m.start_at_one(sp)
            sp.dma_start(idft[:], dram["idft"]).then_inc(idft_in, 16)
            sp.dma_start(bias[:], dram["hyena_bias"]).then_inc(bias_in, 16)

        @block.scalar
        def _(act):
            act.activation(y_hi[:], y_spec[:, :, 0], ACT.Copy).then_inc(hi_done, 1)
            act.wait_ge(idft_in, ONE + 16)
            act.activation(g_hi[:], idft[:], ACT.Copy).then_inc(hi_done, 1)
            act.wait_ge(inv, ONE + CT)
            act.activation(y_hi[:], y_spec[:, :, 1], ACT.Copy).then_inc(hi_done, 1)

        @block.vector
        def _(dve):
            dve.wait_ge(hi_done, ONE + 1)
            dve.tensor_tensor(y_lo[:], y_spec[:, :, 0], f32(y_hi[:]), ALU.subtract).then_inc(lo_done, 1)
            dve.wait_ge(hi_done, ONE + 2)
            dve.tensor_tensor(g_lo[:], idft[:], f32(g_hi[:]), ALU.subtract).then_inc(lo_done, 1)
            dve.wait_ge(bias_in, ONE + 16)
            for n in range(NSEQ * CT):
                s, c = n // CT, n % CT
                if n == CT:
                    dve.wait_ge(hi_done, ONE + 3)
                    dve.tensor_tensor(y_lo[:], y_spec[:, :, 1], f32(y_hi[:]), ALU.subtract).then_inc(lo_done, 1)
                dve.wait_ge(inv, ONE + n + 1)
                z = z_t[:, c, s * L:(s + 1) * L]
                dve.scalar_tensor_tensor(out=z, in0=z, scalar=bias[:, c:c + 1], in1=ps[n % 2][:],
                                         op0=ALU.mult, op1=ALU.add).then_inc(read, 1)

        @block.tensor
        def _(pe):
            for n in range(NSEQ * CT):
                s, c = n // CT, n % CT
                pe.wait_ge(lo_done, ONE + 2 + s)
                if n >= 2:
                    pe.wait_ge(read, ONE + n - 1)
                for k in range(8):
                    last = products(pe, ps[n % 2][:], y_hi[:, k, c * P:(c + 1) * P], y_lo[:, k, c * P:(c + 1) * P],
                                    g_hi[:, k], g_lo[:, k], k == 0, k == 7)
                last.then_inc(inv, 1)


def branches(nc, dram, K, x_hi, x_lo, y_t, br_hi, br_lo):
    with ExitStack() as ctx:
        m = Mem(nc, ctx)
        st = Stream(m, "bw", 2)
        uc = m.sb("b_uc", [P, NSEQ, L])
        W = L + 2 * PAD
        a_pad = m.sb("a_pad", [P, NSEQ, W])
        sums = [m.sb(f"pool_sum{n}", [P, NSEQ, W]) for n in range(2)]
        inv_cnt = m.sb("inv_cnt", [P, L])
        pooled = m.sb("pooled", [P, NSEQ, L])
        pool_w = m.sb("pool_w_sb", [P, CT, P])
        pool_scale = m.sb("pool_scale_sb", [P, CT])
        ps = [m.ps(f"b_ps{b}", [P, NSEQ, L]) for b in range(2)]
        mix = m.ps("mix_ps", [P, NSEQ, L])
        const_in, cnt_in, mid, read, vs, a_in, yb, ybhi = (m.sem(f"b_{n}") for n in (
            "const_in", "cnt_in", "mid", "read", "vs", "a_in", "yb", "ybhi"))
        pooled_done, mixed, mix_hi, mix_lo, zeroed, yblo = (m.sem(f"b_{n}") for n in (
            "pooled", "mixed", "mix_hi", "mix_lo", "zeroed", "yblo"))
        block = ctx.enter_context(nc.Block())

        @block.sync
        def _(sp):
            m.start_at_one(sp)
            sp.dma_start(pool_w[:], dram["pool_w"]).then_inc(const_in, 16)
            sp.dma_start(pool_scale[:], dram["pool_scale"]).then_inc(const_in, 16)
            for j in range(CT):
                for b in range(2):
                    if j:
                        sp.wait_ge(st.lo_done, ONE + 2 * j - 1 + b)
                    sp.dma_start(st.raw[b][:], dram["w_in"][(X0_T, A_T)[b] + j]).then_inc(st.landed[b], 16)
                if j:
                    sp.wait_ge(pooled_done, ONE + j)
                sp.dma_start(inv_cnt[:], dram["inv_cnt"][j:j + 1].broadcast_to([P, L])).then_inc(cnt_in, 16)

        @block.tensor
        def _(pe):
            pe.wait_ge(const_in, ONE + 32)

            def mix_group(g):
                pe.wait_ge(pooled_done, ONE + g + 1)
                if g:
                    pe.wait_ge(mix_lo, ONE + g)
                for s in range(NSEQ):
                    last = pe.matmul(mix[:, s], pool_w[:, g], pooled[:, s], start=True, stop=True)
                last.then_inc(mixed, 1)

            for j in range(CT):
                for b in range(2):
                    pe.wait_ge(st.lo_done, ONE + 2 * j + b + 1)
                    if j:
                        pe.wait_ge((read, a_in)[b], ONE + j)
                    for k in range(KD):
                        c = slice(k * P, (k + 1) * P)
                        for s in range(NSEQ):
                            t = slice(s * L, (s + 1) * L)
                            last = products(pe, ps[b][:, s], st.hi[b][:, c], st.lo[b][:, c], x_hi[:, k, t],
                                            x_lo[:, k, t], k == 0, k == KD - 1)
                    last.then_inc(st.used, 1)
                    if b == 0 and j:
                        mix_group(j - 1)
            mix_group(CT - 1)

        @block.scalar
        def _(act):
            act.wait_ge(const_in, ONE + 32)
            act.wait_ge(zeroed, ONE + 1)

            def after(j):
                col = j
                act.wait_ge(st.used, ONE + 2 * j + 1)
                if j:
                    act.wait_ge(yb, ONE + j)
                act.activation(uc[:], ps[0][:], ACT.Identity, bias=K["conv_b"][:, col:col + 1],
                               scale=K["conv_w"][:, 1, col:col + 1]).then_inc(mid, 1)
                act.wait_ge(st.used, ONE + 2 * j + 2)
                if j:
                    act.wait_ge(pooled_done, ONE + j)
                act.activation(a_pad[:, :, PAD:PAD + L], ps[1][:], ACT.Copy).then_inc(a_in, 1)
                act.wait_ge(yb, ONE + j + 1)
                act.activation(br_hi[:, CT + j], y_t[:, j], ACT.Copy).then_inc(ybhi, 1)
                act.wait_ge(mixed, ONE + j + 1)
                act.activation(br_hi[:, j].rearrange("p (s t) -> p s t", s=NSEQ), mix[:], ACT.Copy,
                               scale=pool_scale[:, j:j + 1]).then_inc(mix_hi, 1)

            def split(n):
                b = n % 2
                act.wait_ge(st.landed[b], ONE + 16 * (n // 2) + 16)
                if n >= 2:
                    act.wait_ge(st.used, ONE + n - 1)
                act.activation(st.hi[b][:], st.raw[b][:], ACT.Copy).then_inc(st.hi_done, 1)

            split(0)
            split(1)
            for j in range(CT):
                if j + 1 < CT:
                    split(2 * j + 2)
                    split(2 * j + 3)
                after(j)

        @block.gpsimd
        def _(pool):
            pool.memset(a_pad[:], 0.0).then_inc(zeroed, 1)

            def split(n):
                b = n % 2
                pool.wait_ge(st.hi_done, ONE + n + 1)
                pool.tensor_tensor(st.lo[b][:], st.raw[b][:], f32(st.hi[b][:]), ALU.subtract).then_inc(st.lo_done, 1)

            split(0)
            split(1)
            for j in range(CT):
                if j + 1 < CT:
                    split(2 * j + 2)
                    split(2 * j + 3)
                pool.wait_ge(ybhi, ONE + j + 1)
                pool.tensor_tensor(br_lo[:, CT + j], y_t[:, j], f32(br_hi[:, CT + j]), ALU.subtract).then_inc(yblo, 1)

        @block.vector
        def _(dve):
            s = Steps(dve, vs, 0, ONE)
            dve.wait_ge(const_in, ONE + 32)
            for j, w in enumerate(WINDOWS):
                dve.wait_ge(mid, ONE + j + 1)
                project_conv(nc, K, 0, ps[0], uc, j, dve, s).then_inc(read, 1)
                dve.wait_ge(read, ONE + j + 1)
                dve.tensor_tensor(y_t[:, j], y_t[:, j], uc[:].rearrange("p s t -> p (s t)"), ALU.mult).then_inc(yb, 1)
                dve.wait_ge(a_in, ONE + j + 1)
                src, width, n = a_pad, 1, 0
                while width < w:
                    span = W - 2 * width + 1
                    s.did(dve.tensor_tensor(sums[n][:, :, 0:span], src[:, :, 0:span], src[:, :, width:width + span],
                                            ALU.add))
                    s.settle()
                    src, width, n = sums[n], 2 * width, 1 - n
                dve.wait_ge(cnt_in, ONE + 16 * (j + 1))
                win = src[:, :, PAD - w // 2:PAD - w // 2 + L]
                if j:
                    dve.wait_ge(mixed, ONE + j)
                for q in range(NSEQ):
                    s.did(dve.tensor_tensor(pooled[:, q], win[:, q], inv_cnt[:], ALU.mult))
                s.settle()
                dve.tensor_tensor(pooled[:], pooled[:], a_pad[:, :, PAD:PAD + L], ALU.subtract).then_inc(pooled_done, 1)
                dve.wait_ge(mix_hi, ONE + j + 1)
                dve.scalar_tensor_tensor(out=br_lo[:, j].rearrange("p (s t) -> p s t", s=NSEQ), in0=mix[:],
                                         scalar=pool_scale[:, j:j + 1],
                                         in1=f32(br_hi[:, j].rearrange("p (s t) -> p s t", s=NSEQ)),
                                         op0=ALU.mult, op1=ALU.subtract).then_inc(mix_lo, 1)


def gated_mix(nc, dram, x_hi, x_lo, br_hi, br_lo):
    with ExitStack() as ctx:
        m = Mem(nc, ctx)
        st = Stream(m, "gw", 3)
        sig = [m.sb(f"sig{b}", [P, NSEQ, L]) for b in range(2)]
        ps = [m.ps(f"g_ps{n}", [P, NSEQ, L]) for n in range(4)]
        mix = m.sb("mix_sb", [P, NSEQ, L])
        sig_done, prod_done, vs, mix_free = m.sem("g_sig"), m.sem("g_prod"), m.sem("g_vs"), m.sem("g_mix_free")
        stored = Mem(nc, ctx).sem("g_stored")
        block = ctx.enter_context(nc.Block())

        @block.sync
        def _(sp):
            m.start_at_one(sp)
            with sp.Fori(0, KD) as i:
                for b in range(3):
                    sp.wait_ge(st.lo_done, ONE + 3 * i)
                    src = dram["w_in"][bass.ds(i + (GA_T, GB_T)[b], 1)] if b < 2 else dram["w_out"][bass.ds(i, 1)]
                    sp.dma_start(st.raw[b][:], src).then_inc(st.landed[b], 16)

        @block.gpsimd
        def _(pool):
            with pool.Fori(0, KD) as i:
                for b in range(3):
                    pool.wait_ge(st.hi_done, ONE + 3 * i + b + 1)
                    pool.tensor_tensor(st.lo[b][:], st.raw[b][:], f32(st.hi[b][:]), ALU.subtract).then_inc(st.lo_done, 1)
                pool.wait_ge(prod_done, ONE + i + 1)
                pool.dma_start(dram["mixed"][bass.ds(i, 1)].rearrange("n s p t -> p (n s) t"),
                               mix[:]).then_inc(stored, 16)
                pool.wait_ge(stored, 16 * i + 16)
                pool.sem_inc(mix_free, 1)

        @block.tensor
        def _(pe):
            with pe.Fori(0, KD) as i:
                for b in range(3):
                    pe.wait_ge(st.lo_done, ONE + 3 * i + b + 1)
                    if b == 0:
                        pe.wait_ge(sig_done, ONE + 2 * i)
                    if b == 2:
                        pe.wait_ge(prod_done, ONE + i)
                    for k in range(KD):
                        c = slice(k * P, (k + 1) * P)
                        for s in range(NSEQ):
                            t = slice(s * L, (s + 1) * L)
                            if b < 2:
                                out, m_hi, m_lo, first, end = ps[b], x_hi, x_lo, k == 0, k == KD - 1
                            else:
                                out, m_hi, m_lo = ps[2 + k // CT], br_hi, br_lo
                                first, end = k % CT == 0, k % CT == CT - 1
                            last = products(pe, out[:, s], st.hi[b][:, c], st.lo[b][:, c], m_hi[:, k, t],
                                            m_lo[:, k, t], first, end)
                    last.then_inc(st.used, 1)

        @block.scalar
        def _(act):
            def split(i, b):
                act.wait_ge(st.landed[b], ONE + 16 * i + 16)
                act.activation(st.hi[b][:], st.raw[b][:], ACT.Copy).then_inc(st.hi_done, 1)

            def turn(i, ahead):
                for b in range(3):
                    if b == 0 or ahead:
                        act.wait_ge(st.used, ONE + 3 * i + b)
                        split(i + (b + 2) // 3, (b + 2) % 3)
                    if b < 2:
                        act.wait_ge(st.used, ONE + 3 * i + b + 1)
                        act.wait_ge(prod_done, ONE + i)
                        act.activation(sig[b][:], ps[b][:], ACT.Sigmoid).then_inc(sig_done, 1)

            split(0, 0)
            split(0, 1)
            with act.Fori(0, KD - 1) as i:
                turn(i, True)
            turn(KD - 1, False)

        @block.vector
        def _(dve):
            with dve.Fori(0, KD) as i:
                s = Steps(dve, vs, 2 * i, ONE)
                dve.wait_ge(st.used, ONE + 3 * i + 3)
                for b in range(2):
                    dve.wait_ge(sig_done, ONE + 2 * i + b + 1)
                    s.did(dve.tensor_tensor(sig[b][:], sig[b][:], ps[2 + b][:], ALU.mult))
                s.settle()
                dve.wait_ge(mix_free, ONE + i)
                dve.tensor_tensor(mix[:], sig[0][:], sig[1][:], ALU.add).then_inc(prod_done, 1)


def residual(nc, dram, h):
    with ExitStack() as ctx:
        m = Mem(nc, ctx)
        st = Stream(m, "ow", 2)
        m_raw = [m.sb(f"m_raw{b}", [P, L]) for b in range(2)]
        m_in = [m.sem(f"m_in{b}") for b in range(2)]
        m_hi = [m.sb(f"m_hi{b}", [P, L], F32R) for b in range(2)]
        m_lo = [m.sb(f"m_lo{b}", [P, L], F32R) for b in range(2)]
        ps = [[m.ps(f"h_ps{t}_{n}", [P, 512]) for n in range(2)] for t in range(LT)]
        x_in, mhi, mlo, added = (m.sem(f"h_{n}") for n in ("x_in", "mhi", "mlo", "added"))
        block = ctx.enter_context(nc.Block())
        NJ = LT * 2

        @block.sync
        def _(sp):
            m.start_at_one(sp)
            for s in range(NSEQ):
                sp.dma_start(h[:, s * LT:(s + 1) * LT], dram["x"][s]).then_inc(x_in, 16)
            for s in range(NSEQ):
                with sp.Fori(0, KD // 2) as i:
                    for b in range(2):
                        sp.wait_ge(st.lo_done, ONE + s * KD + 2 * i)
                        sp.dma_start(st.raw[b][:], dram["w_o"][bass.ds(2 * i + b, 1)]).then_inc(st.landed[b], 16)
                        sp.wait_ge(mlo, ONE + s * KD + 2 * i)
                        sp.dma_start(m_raw[b][:], dram["mixed"][bass.ds(2 * i + b, 1), s]).then_inc(m_in[b], 16)

        @block.scalar
        def _(act):
            for s in range(NSEQ):
                with act.Fori(0, KD // 2) as i:
                    for b in range(2):
                        act.wait_ge(st.landed[b], ONE + 16 * (s * KD // 2 + i + 1))
                        act.wait_ge(st.used, ONE + s * KD + 2 * i)
                        act.activation(st.hi[b][:], st.raw[b][:], ACT.Copy).then_inc(st.hi_done, 1)
                        act.wait_ge(m_in[b], ONE + 16 * (s * KD // 2 + i + 1))
                        act.activation(m_hi[b][:], m_raw[b][:], ACT.Copy).then_inc(mhi, 1)

        @block.gpsimd
        def _(pool):
            for s in range(NSEQ):
                with pool.Fori(0, KD // 2) as i:
                    for b in range(2):
                        pool.wait_ge(st.hi_done, ONE + s * KD + 2 * i + b + 1)
                        pool.tensor_tensor(st.lo[b][:], st.raw[b][:], f32(st.hi[b][:]), ALU.subtract).then_inc(st.lo_done, 1)

        @block.vector
        def _(dve):
            dve.wait_ge(x_in, ONE + 32)
            for s in range(NSEQ):
                with dve.Fori(0, KD // 2) as i:
                    for b in range(2):
                        dve.wait_ge(mhi, ONE + s * KD + 2 * i + b + 1)
                        dve.tensor_tensor(m_lo[b][:], m_raw[b][:], f32(m_hi[b][:]), ALU.subtract).then_inc(mlo, 1)
                dve.wait_ge(st.used, ONE + (s + 1) * KD)
                for t in range(LT):
                    for n in range(2):
                        part = h[:, s * LT + t, n * 512:(n + 1) * 512]
                        dve.tensor_tensor(part, part, ps[t][n][:], ALU.add).then_inc(added, 1)

        @block.tensor
        def _(pe):
            def chunk(s, i, b, first, end):
                pe.wait_ge(st.lo_done, ONE + s * KD + 2 * i + b + 1)
                pe.wait_ge(mlo, ONE + s * KD + 2 * i + b + 1)
                for t in range(LT):
                    if first and s:
                        pe.wait_ge(added, ONE + NJ * (s - 1) + 2 * t + 2)
                    for n in range(2):
                        c = slice(n * 512, (n + 1) * 512)
                        w = slice(t * P, (t + 1) * P)
                        last = products(pe, ps[t][n][:], m_hi[b][:, w], m_lo[b][:, w], st.hi[b][:, c],
                                        st.lo[b][:, c], first, end)
                last.then_inc(st.used, 1)

            for s in range(NSEQ):
                chunk(s, 0, 0, True, False)
                chunk(s, 0, 1, False, False)
                with pe.Fori(1, KD // 2 - 1) as i:
                    chunk(s, i, 0, False, False)
                    chunk(s, i, 1, False, False)
                chunk(s, KD // 2 - 1, 0, False, False)
                chunk(s, KD // 2 - 1, 1, False, True)


def key_scores(nc, dram, x_hi, x_lo):
    with ExitStack() as ctx:
        m = Mem(nc, ctx)
        st = Stream(m, "qw", 2)
        keys = m.sb("keys", [P, 2 * H, NK])
        k_hi, k_lo = m.sb("keys_hi", [P, 2 * H, NK], F32R), m.sb("keys_lo", [P, 2 * H, NK], F32R)
        q_hi = [m.sb(f"q_hi{b}", [P, T], F32R) for b in range(2)]
        q_lo = [m.sb(f"q_lo{b}", [P, T], F32R) for b in range(2)]
        sc = m.sb("head_scores", [P, TT, 2, NK])
        q_ps = [m.ps(f"q_ps{b}", [P, NSEQ, L]) for b in range(2)]
        s_ps = [m.ps(f"s_ps{b}", [P, TT, NK]) for b in range(2)]
        keys_in, keys_hi_done, keys_lo_done, qhi, qlo, scored, read, sc_free = (m.sem(f"q_{n}") for n in (
            "keys_in", "keys_hi", "keys_lo", "hi", "lo", "scored", "read", "sc_free"))
        stored = Mem(nc, ctx).sem("q_stored")
        block = ctx.enter_context(nc.Block())

        @block.sync
        def _(sp):
            m.start_at_one(sp)
            sp.dma_start(keys[:], dram["keys"]).then_inc(keys_in, 16)
            with sp.Fori(0, H) as i:
                for b in range(2):
                    sp.wait_ge(st.lo_done, ONE + 2 * i)
                    sp.dma_start(st.raw[b][:], dram["wq"][bass.ds(2 * i + b, 1)]).then_inc(st.landed[b], 16)

        @block.gpsimd
        def _(pool):
            with pool.Fori(0, H) as i:
                for b in range(2):
                    pool.wait_ge(st.hi_done, ONE + 2 * i + b + 1)
                    pool.tensor_tensor(st.lo[b][:], st.raw[b][:], f32(st.hi[b][:]), ALU.subtract).then_inc(st.lo_done, 1)
                pool.wait_ge(read, ONE + 2 * i + 2)
                pool.dma_start(dram["scores"][:, bass.ds(i, 1)].rearrange("n h p k -> p (n h) k"),
                               sc[:].rearrange("p n h k -> p n (h k)")).then_inc(stored, 16)
                pool.wait_ge(stored, 16 * i + 16)
                pool.sem_inc(sc_free, 1)

        @block.scalar
        def _(act):
            act.wait_ge(keys_in, ONE + 16)
            act.activation(k_hi[:], keys[:], ACT.Copy).then_inc(keys_hi_done, 1)

            def turn(i, b, ahead):
                if ahead:
                    split_next(act, st, i, b)
                act.wait_ge(st.used, ONE + 2 * i + b + 1)
                act.wait_ge(scored, ONE + 2 * i)
                act.activation(q_hi[b][:], q_ps[b][:].rearrange("p s t -> p (s t)"), ACT.Copy).then_inc(qhi, 1)

            split_first(act, st)
            with act.Fori(0, H - 1) as i:
                for b in range(2):
                    turn(i, b, True)
            turn(H - 1, 0, True)
            turn(H - 1, 1, False)

        @block.vector
        def _(dve):
            dve.wait_ge(keys_hi_done, ONE + 1)
            dve.tensor_tensor(k_lo[:], keys[:], f32(k_hi[:]), ALU.subtract).then_inc(keys_lo_done, 1)
            with dve.Fori(0, H) as i:
                for b in range(2):
                    dve.wait_ge(qhi, ONE + 2 * i + b + 1)
                    dve.tensor_tensor(q_lo[b][:], q_ps[b][:].rearrange("p s t -> p (s t)"), f32(q_hi[b][:]),
                                      ALU.subtract).then_inc(qlo, 1)
                for b in range(2):
                    dve.wait_ge(scored, ONE + 2 * i + b + 1)
                    dve.wait_ge(sc_free, ONE + i)
                    dve.tensor_copy(sc[:, :, b], s_ps[b][:]).then_inc(read, 1)

        @block.tensor
        def _(pe):
            pe.wait_ge(keys_lo_done, ONE + 1)
            with pe.Fori(0, H) as i:
                for b in range(2):
                    pe.wait_ge(st.lo_done, ONE + 2 * i + b + 1)
                    pe.wait_ge(qlo, ONE + 2 * i)
                    for k in range(KD):
                        c = slice(k * P, (k + 1) * P)
                        for s in range(NSEQ):
                            t = slice(s * L, (s + 1) * L)
                            last = products(pe, q_ps[b][:, s], st.hi[b][:, c], st.lo[b][:, c], x_hi[:, k, t],
                                            x_lo[:, k, t], k == 0, k == KD - 1)
                    last.then_inc(st.used, 1)
                for b in range(2):
                    pe.wait_ge(qlo, ONE + 2 * i + b + 1)
                    pe.wait_ge(read, ONE + 2 * i)
                    for t in range(TT):
                        c = slice(t * P, (t + 1) * P)
                        hp = bass.ds(2 * i + b, 1)
                        last = products(pe, s_ps[b][:, t], q_hi[b][:, c], q_lo[b][:, c],
                                        k_hi[:, hp].rearrange("p h k -> p (h k)"),
                                        k_lo[:, hp].rearrange("p h k -> p (h k)"), True, True)
                    last.then_inc(scored, 1)


def experts_in(nc, dram, x_hi, x_lo):
    with ExitStack() as ctx:
        m = Mem(nc, ctx)
        st = Stream(m, "uw", 2)
        gel = [m.sb(f"gel{b}", [P, T]) for b in range(2)]
        sc = [m.sb(f"sc{b}", [P, 2, NK]) for b in range(2)]
        rest = [m.sb(f"rest{p}", [P, NK]) for p in range(2)]
        carrier = m.sb("carrier", [P, 2])
        top = m.sb("top", [P, 2, TOPK])
        top_at = m.sb("top_at", [P, 2, TOPK], U32)
        top_key = m.sb("top_key", [P, 2, TOPK])
        pairs = m.sb("pairs", [P, TOPK, TOPK])
        pairs_rest = m.sb("pairs_rest", [P, TOPK * TOPK])
        best = m.sb("best", [P, TOPK])
        best_at = m.sb("best_at", [P, TOPK], U32)
        rank_u = m.sb("rank_u", [P, 2, TOPK], U32)
        rank = m.sb("rank", [P, 2, TOPK])
        pick = [m.sb(f"pick{p}", [P, TOPK, TOPK]) for p in range(2)]
        sel = m.sb("sel", [P, 3, P])
        gate_exp = m.sb("gate_exp", [P, H, TOPK])
        gate_sum = m.sb("gate_sum", [P, H])
        sel_t = m.sb("sel_t", [P, 3, P])
        iota = m.sb("iota", [P, P])
        ident = m.sb("e_ident", [P, P])
        hot_i = [m.sb(f"hot_i{c}", [P, 8, P]) for c in range(2)]
        hot_j = [m.sb(f"hot_j{c}", [P, 8, P]) for c in range(2)]
        stage = [m.sb(f"stage{f}", [P, P, 64]) for f in range(2)]
        s_ps = [m.ps(f"e_ps{b}", [P, NSEQ, L]) for b in range(2)]
        g_ps = [m.ps(f"gate_ps{b}", [P, 4, P]) for b in range(2)]
        tr_ps = m.ps("tr_ps", [P, 3, P])
        const_in = m.sem("e_const_in")
        sc_in = [m.sem(f"e_sc_in{b}") for b in range(2)]
        gel_done = m.sem("e_gel_done")
        gel_stored = [m.sem(f"e_gel_stored{b}") for b in range(2)]
        gate_stored = [m.sem(f"e_gate_stored{f}") for f in range(2)]
        routed, exp_done, sel_done, turned, sel_t_done = (m.sem(f"e_{n}") for n in (
            "routed", "exp_done", "sel_done", "turned", "sel_t_done"))
        hot_done = [m.sem(f"e_hot_done{c}") for c in range(2)]
        gates_done = m.sem("e_gates_done")
        gates_read = [m.sem(f"e_gates_read{b}") for b in range(2)]
        vs = m.sem("e_vs")
        block = ctx.enter_context(nc.Block())
        ROUTE_STEPS = 34
        EDGE_STEPS = 3

        def steps_of_tile(eng, body):
            for half in range(2):
                with eng.Fori(0, 2) as q:
                    for e in range(2):
                        body(half * 4 + 2 * q + e, q, half, e)

        @block.sync
        def _(sp):
            m.start_at_one(sp)
            sp.dma_start(iota[:], dram["iota"]).then_inc(const_in, 16)
            sp.dma_start(ident[:], dram["ident"]).then_inc(const_in, 16)

            def load_scores(r, e):
                sp.wait_ge(routed, ONE + r - e)
                sp.dma_start(sc[e][:].rearrange("p h k -> p (h k)"),
                             dram["scores_flat"][bass.ds(r, 1)]).then_inc(sc_in[e], 16)

            def load_u(n):
                for b in range(2):
                    sp.wait_ge(st.lo_done, ONE + 2 * n)
                    sp.dma_start(st.raw[b][:], dram["peer_u"][bass.ds(2 * n + b, 1)]).then_inc(st.landed[b], 16)

            with sp.Fori(0, H // 2) as q:
                for e in range(2):
                    load_scores(2 * q + e, e)
            with sp.Fori(0, TT - 1) as tt:
                def body(h, q, half, e):
                    load_u(tt * H + h)
                    load_scores((tt + 1) * H + h, e)
                steps_of_tile(sp, body)
            steps_of_tile(sp, lambda h, q, half, e: load_u((TT - 1) * H + h))

        @block.gpsimd
        def _(pool):
            with pool.Fori(0, P // 2) as i:
                for b in range(2):
                    pool.wait_ge(st.hi_done, ONE + 2 * i + b + 1)
                    pool.tensor_tensor(st.lo[b][:], st.raw[b][:], f32(st.hi[b][:]), ALU.subtract).then_inc(st.lo_done, 1)

        @block.tensor
        def _(pe):
            pe.wait_ge(const_in, ONE + 32)
            with pe.Fori(0, TT) as tt:
                pe.wait_ge(sel_done, ONE + tt + 1)
                for a in range(3):
                    t = pe.transpose(tr_ps[:, a], sel[:, a], ident[:])
                t.then_inc(turned, 1)

                def body(h, q, half, e):
                    n = tt * H + h
                    for b in range(2):
                        pe.wait_ge(st.lo_done, ONE + 2 * n + b + 1)
                        pe.wait_ge(gel_done, ONE + 2 * n)
                        for k in range(KD):
                            c = slice(k * P, (k + 1) * P)
                            for s in range(NSEQ):
                                t = slice(s * L, (s + 1) * L)
                                last = products(pe, s_ps[b][:, s], st.hi[b][:, c], st.lo[b][:, c], x_hi[:, k, t],
                                                x_lo[:, k, t], k == 0, k == KD - 1)
                        last.then_inc(st.used, 1)
                        pe.wait_ge(hot_done[b], ONE + n + 1)
                        for u in range(2):
                            pe.wait_ge(gates_read[u], ONE + 2 * n + b)
                            for v in range(4):
                                g = pe.matmul(g_ps[u][:, v], hot_i[b][:, 4 * u + v], hot_j[b][:, 4 * u + v],
                                              start=True, stop=True)
                            g.then_inc(gates_done, 1)

                steps_of_tile(pe, body)

        @block.scalar
        def _(act):
            def step(tt, h, half, e, final=False):
                n = tt * H + h
                for b in range(2):
                    if not (final and b):
                        split_next(act, st, n, b)
                    act.wait_ge(st.used, ONE + 2 * n + b + 1)
                    act.wait_ge(gel_stored[b], ONE + 16 * n)
                    act.activation(gel[b][:], s_ps[b][:].rearrange("p s t -> p (s t)"),
                                   ACT.Gelu_apprx_tanh).then_inc(gel_done, 1)
                    for u in range(2):
                        act.wait_ge(gates_done, ONE + 4 * n + 2 * b + u + 1)
                        t0 = (h - 4 * half) * 16 + 8 * b + 4 * u
                        act.activation(stage[half][:, :, bass.ds(t0, 4)], g_ps[u][:].rearrange("p t j -> p j t"),
                                       ACT.Copy).then_inc(gates_read[u], 1)
                    act.wait_ge(gel_done, ONE + 2 * n + b + 1)
                    act.dma_start(dram["act"][bass.ds(2 * n + b, 1)], gel[b][:]).then_inc(gel_stored[b], 16)

            def token_tile(tt, final):
                act.wait_ge(routed, ONE + (tt + 1) * H)
                act.activation(gate_exp[:], sel[:, 2].rearrange("p (h r) -> p h r", h=H), ACT.Exp).then_inc(exp_done, 1)
                for half in range(2):
                    act.wait_ge(gate_stored[half], ONE + 16 * tt)
                    if final and half:
                        for q in range(2):
                            for e in range(2):
                                step(tt, half * 4 + 2 * q + e, half, e, q == 1 and e == 1)
                    else:
                        with act.Fori(0, 2) as q:
                            for e in range(2):
                                step(tt, half * 4 + 2 * q + e, half, e)
                    for u in range(2):
                        act.wait_ge(gates_read[u], ONE + 16 * tt + 8 * half + 8)
                    act.dma_start(dram["gates"][bass.ds(2 * tt + half, 1)],
                                  stage[half][:].rearrange("p j t -> p (j t)")).then_inc(gate_stored[half], 16)

            split_first(act, st)
            with act.Fori(0, TT - 1) as tt:
                token_tile(tt, False)
            token_tile(TT - 1, True)
            for b in range(2):
                act.wait_ge(gel_stored[b], ONE + 16 * (P // 2))
                act.wait_ge(gate_stored[b], ONE + 16 * TT)

        @block.vector
        def _(dve):
            def carry_wait(at=0):
                return dve.tensor_copy(carrier[:, at:at + 1], iota[:, 0:1])

            def route(r, h, e, sc_turn, base):
                s = Steps(dve, vs, base, ONE)
                out = bass.ds(h * TOPK, TOPK)
                dve.wait_ge(sc_in[e], ONE + 16 * sc_turn + 16)
                s.did(carry_wait())
                for p in range(2):
                    s.did(dve.max(top[:, p, 0:8], sc[e][:, p]))
                s.settle()
                s.did(carry_wait())
                for p in range(2):
                    s.did(dve.match_replace(rest[p][:], top[:, p, 0:8], sc[e][:, p], LOWEST))
                    s.did(dve.max_index(top_at[:, p, 0:8], top[:, p, 0:8], sc[e][:, p]))
                s.settle()
                s.did(carry_wait())
                for p in range(2):
                    s.did(dve.max(top[:, p, 8:16], rest[p][:]))
                s.settle()
                s.did(carry_wait())
                for p in range(2):
                    s.did(dve.max_index(top_at[:, p, 8:16], top[:, p, 8:16], rest[p][:]))
                s.did(dve.tensor_tensor(pairs[:], top[:, 0].unsqueeze(2).broadcast_to([P, TOPK, TOPK]),
                                        top[:, 1].unsqueeze(1).broadcast_to([P, TOPK, TOPK]), ALU.add))
                s.settle()
                flat = pairs[:].rearrange("p a b -> p (a b)")
                s.did(dve.tensor_copy(top_key[:], top_at[:]))
                s.did(dve.max(best[:, 0:8], flat))
                s.settle()
                s.did(carry_wait())
                s.did(dve.match_replace(pairs_rest[:], best[:, 0:8], flat, LOWEST))
                s.did(dve.max_index(best_at[:, 0:8], best[:, 0:8], flat))
                s.settle()
                s.did(carry_wait())
                s.did(dve.max(best[:, 8:16], pairs_rest[:]))
                s.settle()
                s.did(carry_wait())
                s.did(dve.max_index(best_at[:, 8:16], best[:, 8:16], pairs_rest[:]))
                s.settle()
                s.did(dve.tensor_scalar(rank_u[:, 0], best_at[:], 4, None, ALU.logical_shift_right))
                s.did(dve.tensor_scalar(rank_u[:, 1], best_at[:], TOPK - 1, None, ALU.bitwise_and))
                s.did(dve.tensor_scalar(sel[:, 2, out], best[:], best[:, 0:1], None, ALU.subtract))
                s.settle()
                s.did(dve.tensor_copy(rank[:], rank_u[:]))
                s.settle()
                for p in range(2):
                    s.did(dve.tensor_tensor(pick[p][:], rank[:, p].unsqueeze(2).broadcast_to([P, TOPK, TOPK]),
                                            iota[:, 0:TOPK].unsqueeze(1).broadcast_to([P, TOPK, TOPK]), ALU.is_equal))
                s.settle()
                for p in range(2):
                    s.did(dve.tensor_tensor(pick[p][:], pick[p][:],
                                            top_key[:, p].unsqueeze(1).broadcast_to([P, TOPK, TOPK]), ALU.mult))
                s.settle()
                s.did(dve.tensor_reduce(sel[:, 0, out], pick[0][:], X, ALU.add))
                s.did(dve.tensor_reduce(sel[:, 1, out], pick[1][:], X, ALU.add))
                assert s.n == ROUTE_STEPS, s.n
                s.settle()
                dve.sem_inc(routed, 1)

            def build(n, h, c):
                dve.wait_ge(gates_done, ONE + 4 * n)
                for v in range(8):
                    t = h * 16 + 8 * c + v
                    dve.tensor_scalar(hot_i[c][:, v], iota[:], sel_t[:, 0, bass.ds(t, 1)], None, ALU.is_equal)
                    last = dve.tensor_scalar(hot_j[c][:, v], iota[:], sel_t[:, 1, bass.ds(t, 1)],
                                             sel_t[:, 2, bass.ds(t, 1)], ALU.is_equal, ALU.mult)
                last.then_inc(hot_done[c], 1)

            def edge(tt, base):
                s = Steps(dve, vs, base, ONE)
                dve.wait_ge(exp_done, ONE + tt + 1)
                s.did(dve.tensor_reduce(gate_sum[:], gate_exp[:], X, ALU.add))
                s.settle()
                s.did(dve.reciprocal(gate_sum[:], gate_sum[:]))
                s.settle()
                dve.tensor_tensor(sel[:, 2].rearrange("p (h r) -> p h r", h=H), gate_exp[:],
                                  gate_sum[:].unsqueeze(2).broadcast_to([P, H, TOPK]), ALU.mult).then_inc(sel_done, 1)
                dve.wait_ge(turned, ONE + tt + 1)
                dve.tensor_copy(sel_t[:], tr_ps[:]).then_inc(sel_t_done, 1)
                dve.wait_ge(sel_t_done, ONE + tt + 1)
                s.did(carry_wait(1))

            dve.wait_ge(const_in, ONE + 32)
            with dve.Fori(0, H // 2) as q:
                for e in range(2):
                    route(2 * q + e, 2 * q + e, e, q, (2 * q + e) * ROUTE_STEPS)
            with dve.Fori(0, TT - 1) as tt:
                edge(tt, (tt + 1) * (H * ROUTE_STEPS) + tt * EDGE_STEPS)

                def body(h, q, half, e):
                    n = tt * H + h
                    for c in range(2):
                        build(n, h, c)
                    route(n + H, h, e, (tt + 1) * 4 + 2 * half + q, (n + H) * ROUTE_STEPS + (tt + 1) * EDGE_STEPS)

                steps_of_tile(dve, body)
            edge(TT - 1, TT * H * ROUTE_STEPS + (TT - 1) * EDGE_STEPS)

            def body(h, q, half, e):
                for c in range(2):
                    build((TT - 1) * H + h, h, c)

            steps_of_tile(dve, body)


def experts_out(nc, dram, out):
    GJ = 4
    NG = P // GJ
    with ExitStack() as ctx:
        m = Mem(nc, ctx)
        acc = m.sb("acc", [P, TT, D])
        a_raw = [m.sb(f"a_raw{b}", [P, T // 64, 64]) for b in range(2)]
        g_raw = [m.sb(f"g_raw{b}", [P, T // 64, 2 * 64]) for b in range(2)]
        v_raw = [m.sb(f"v_raw{b}", [P, D]) for b in range(2)]
        a_hi = [m.sb(f"a_hi{g}", [P, GJ, T], F32R) for g in range(2)]
        a_lo = [m.sb(f"a_lo{g}", [P, GJ, T], F32R) for g in range(2)]
        v_hi = [m.sb(f"v_hi{g}", [P, GJ, D], F32R) for g in range(2)]
        v_lo = [m.sb(f"v_lo{g}", [P, GJ, D], F32R) for g in range(2)]
        ps = [m.ps(f"o_ps{n}", [P, 512]) for n in range(8)]
        h_in, a_in, g_in, v_in = (m.sem("o_h_in"), [m.sem(f"o_a_in{b}") for b in range(2)],
                                  [m.sem(f"o_g_in{b}") for b in range(2)], [m.sem(f"o_v_in{b}") for b in range(2)])
        gated, ahi, alo, vhi, vlo, summed, bank_free = (m.sem(f"o_{n}") for n in (
            "gated", "ahi", "alo", "vhi", "vlo", "summed", "bank_free"))
        gain_in, squared, ms, root, inv, normed, stored = (m.sem(f"o_{n}") for n in (
            "gain_in", "squared", "ms", "root", "inv", "normed", "stored"))
        block = ctx.enter_context(nc.Block())
        JOBS = TT * 2

        @block.sync
        def _(sp):
            m.start_at_one(sp)
            sp.dma_start(acc[:].rearrange("p n d -> p (n d)"), dram["h"]).then_inc(h_in, 16)
            with sp.Fori(0, P // 4) as g:
                for pair in range(2):
                    i = 2 * g + pair
                    sp.wait_ge(gated, ONE + 4 * g)
                    sp.dma_start(g_raw[pair][:], dram["gates"].rearrange("b i (j t) -> i b j t", t=64)[
                        :, :, bass.ds(2 * i, 2)].rearrange("i b j t -> i b (j t)")).then_inc(g_in[pair], 16)
                    for b in range(2):
                        sp.wait_ge(alo, ONE + 2 * i)
                        sp.dma_start(a_raw[b][:].rearrange("p a t -> p (a t)"),
                                     dram["act"][bass.ds(2 * i + b, 1)]).then_inc(a_in[b], 16)
                        sp.wait_ge(vlo, ONE + 2 * i)
                        sp.dma_start(v_raw[b][:], dram["peer_v"][bass.ds(2 * i + b, 1)]).then_inc(v_in[b], 16)
            gain = v_raw[0]
            sp.wait_ge(vlo, ONE + P)
            sp.dma_start(gain[:], dram["normf_g"].broadcast_to([P, D])).then_inc(gain_in, 16)
            sp.wait_ge(normed, ONE + TT)
            for s in range(NSEQ):
                sp.dma_start(out[s].rearrange("(n p) d -> p n d", p=P), acc[:, s * LT:(s + 1) * LT]).then_inc(stored, 16)
            sp.wait_ge(stored, ONE + 16 * NSEQ)

        def each_group(eng, body, first=0, last=NG):
            with eng.Fori(0, (last - first) // 2) as i:
                for w in range(2):
                    body(2 * i + first + w, w)
            if (last - first) % 2:
                body(last - 1, 0)

        @block.gpsimd
        def _(pool):
            def body(g, w):
                for k in range(GJ):
                    pool.wait_ge(vhi, ONE + 4 * g + k + 1)
                    pool.tensor_tensor(v_lo[w][:, k], v_raw[k % 2][:], f32(v_hi[w][:, k]), ALU.subtract).then_inc(vlo, 1)
            each_group(pool, body)

        @block.scalar
        def _(act):
            def body(g, w):
                for k in range(GJ):
                    if k == 0:
                        act.wait_ge(summed, ONE + JOBS * (g + 1))
                    act.wait_ge(v_in[k % 2], ONE + 16 * (2 * g + k // 2) + 16)
                    act.activation(v_hi[w][:, k], v_raw[k % 2][:], ACT.Copy).then_inc(vhi, 1)
                    act.wait_ge(gated, ONE + 4 * g + k + 1)
                    act.activation(a_hi[w][:, k], a_raw[k % 2][:].rearrange("p a t -> p (a t)"), ACT.Copy).then_inc(ahi, 1)
            each_group(act, body)
            act.wait_ge(bank_free, ONE + NG * JOBS + 8)
            sq = g_raw[0][:].rearrange("p a t -> p (a t)")[:, 0:D]
            ss = g_raw[1][:, 0, 0:TT]
            for tt in range(TT):
                if tt:
                    act.wait_ge(squared, ONE + tt)
                act.activation(sq, acc[:, tt], ACT.Square, accum_out=ss[:, tt:tt + 1]).then_inc(squared, 1)
            act.wait_ge(ms, ONE + 1)
            act.activation(ss, ss, ACT.Sqrt).then_inc(root, 1)

        @block.vector
        def _(dve):
            def prepare(g, w, k):
                b = k % 2
                dve.wait_ge(a_in[b], ONE + 16 * (2 * g + k // 2) + 16)
                if b == 0:
                    dve.wait_ge(g_in[k // 2], ONE + 16 * g + 16)
                dve.tensor_tensor(a_raw[b][:], a_raw[b][:], g_raw[k // 2][:, :, b * 64:(b + 1) * 64],
                                  ALU.mult).then_inc(gated, 1)
                dve.wait_ge(ahi, ONE + 4 * g + k + 1)
                dve.tensor_tensor(a_lo[w][:, k], a_raw[b][:].rearrange("p a t -> p (a t)"), f32(a_hi[w][:, k]),
                                  ALU.subtract).then_inc(alo, 1)

            def add(g, k):
                for n in range(4 * k, 4 * k + 4):
                    dve.wait_ge(summed, ONE + JOBS * (g + 2) + n + 1)
                    part = acc[:, n // 2, n % 2 * 512:(n % 2 + 1) * 512]
                    dve.tensor_tensor(part, part, ps[n % 8][:], ALU.add).then_inc(bank_free, 1)

            dve.nop().then_inc(bank_free, 8)
            dve.wait_ge(h_in, ONE + 16)
            for k in range(GJ):
                prepare(0, 0, k)

            def body(g, w):
                for k in range(GJ):
                    prepare(g + 1, 1 - w, k)
                    add(g, k)

            each_group(dve, body, 0, NG - 1)
            for k in range(GJ):
                add(NG - 1, k)
            ss = g_raw[1][:, 0, 0:TT]
            dve.wait_ge(squared, ONE + TT)
            dve.tensor_scalar(ss, ss, 1.0 / D, EPS, ALU.mult, ALU.add).then_inc(ms, 1)
            dve.wait_ge(root, ONE + 1)
            dve.reciprocal(ss, ss).then_inc(inv, 1)
            dve.wait_ge(inv, ONE + 1)
            dve.wait_ge(gain_in, ONE + 16)
            for tt in range(TT):
                dve.scalar_tensor_tensor(out=acc[:, tt], in0=acc[:, tt], scalar=ss[:, tt:tt + 1], in1=v_raw[0][:],
                                         op0=ALU.mult, op1=ALU.mult).then_inc(normed, 1)

        @block.tensor
        def _(pe):
            pe.nop().then_inc(summed, 2 * JOBS)

            def body(g, w):
                pe.wait_ge(alo, ONE + 4 * g + 4)
                pe.wait_ge(vlo, ONE + 4 * g + 4)
                for n in range(JOBS):
                    tt, c = n // 2, slice(n % 2 * 512, (n % 2 + 1) * 512)
                    t = slice(tt * P, (tt + 1) * P)
                    pe.wait_ge(bank_free, ONE + JOBS * g + n + 1)
                    for k in range(GJ):
                        last = products(pe, ps[n % 8][:], a_hi[w][:, k, t], a_lo[w][:, k, t], v_hi[w][:, k, c],
                                        v_lo[w][:, k, c], k == 0, k == GJ - 1)
                    last.then_inc(summed, 1)
            each_group(pe, body)



def program(nc, dram, out):
    with ExitStack() as x_ctx, ExitStack() as branch_ctx:
        with ExitStack() as k_ctx:
            k = Mem(nc, k_ctx, "right")
            K = {"dft_hi": k.sb("dft_hi", [P, LT, N_FFT], F32R), "dft_lo": k.sb("dft_lo", [P, LT, N_FFT], F32R),
                 "k_re": k.sb("k_re", [P, 4, C]), "k_im": k.sb("k_im", [P, 4, C]), "k_re0": k.sb("k_re0", [P, C])}
            filters(nc, dram, K)
            x = Mem(nc, x_ctx)
            K["conv_w"], K["conv_b"] = x.sb("conv_w_sb", [P, 3, 12]), x.sb("conv_b_sb", [P, 12])
            x_hi, x_lo = x.sb("xn_hi", [P, KD, T], F32R), x.sb("xn_lo", [P, KD, T], F32R)
            with ExitStack() as ctx:
                src = Mem(nc, ctx).sb("x_sb", [P, TT, D])
                norm_transpose(nc, dram, "n1", dram["x"], src, "norm1_g", None, x_hi, x_lo)
            z_t = Mem(nc, x_ctx).sb("z_t", [P, CT, T])
            y_ctx = ExitStack()
            y_spec = Mem(nc, y_ctx).sb("y_spec", [P, 8, NSEQ, C])
            gate_product(nc, dram, K, x_hi, x_lo, z_t)
            forward_dft(nc, dram, K, z_t, y_spec)
        inverse_dft(nc, dram, y_spec, z_t)
        y_ctx.close()
        b = Mem(nc, branch_ctx, "right")
        br_hi, br_lo = b.sb("br_hi", [P, 8, T], F32R), b.sb("br_lo", [P, 8, T], F32R)
        branches(nc, dram, K, x_hi, x_lo, z_t, br_hi, br_lo)
        gated_mix(nc, dram, x_hi, x_lo, br_hi, br_lo)
    with ExitStack() as x_ctx:
        x = Mem(nc, x_ctx, "right")
        x_hi, x_lo = x.sb("xb_hi", [P, KD, T], F32R), x.sb("xb_lo", [P, KD, T], F32R)
        with ExitStack() as ctx:
            h = Mem(nc, ctx).sb("h_sb", [P, TT, D])
            residual(nc, dram, h)
            norm_transpose(nc, dram, "n2", None, h, "norm2_g", dram["h"], x_hi, x_lo)
        key_scores(nc, dram, x_hi, x_lo)
        experts_in(nc, dram, x_hi, x_lo)
    experts_out(nc, dram, out)


def constants():
    f64 = np.float64
    t = np.linspace(0.0, 1.0, L, dtype=np.float32).astype(f64)
    bands = (FEMB - 1) // 2
    wpos = (2.0 * np.pi * np.arange(L) / L).astype(np.float32)
    freqs = np.linspace(1e-4, bands - 1, bands).astype(np.float32)
    ang = (freqs[:, None] * wpos[None, :]).astype(np.float32).astype(f64)
    pos = np.concatenate([t[None, :], np.cos(ang), -np.sin(ang)], axis=0)
    lo, hi = np.log(1e-2) / 1.5, np.log(1e-2) / 0.3
    decay = np.exp(-t[:, None] * np.abs(np.linspace(lo, hi, C))[None, :])
    grid = 2.0 * np.pi * (np.outer(np.arange(L), np.arange(L)) % N_FFT) / N_FFT
    fwd = np.concatenate([np.cos(grid), -np.sin(grid)], axis=1)
    fwd[:, L] = (-1.0) ** np.arange(L)
    inv = fwd.T * (2.0 / N_FFT)
    inv[0] /= 2
    inv[L] /= 2
    n = np.arange(L)
    cnt = np.stack([np.minimum(n + w // 2, L) - np.maximum(n - w // 2, 0) for w in WINDOWS])

    def tiles(a):
        return a.reshape(-1, P, a.shape[-1]).transpose(1, 0, 2)

    f = lambda a: np.ascontiguousarray(a, dtype=np.float32)
    return {"filt_pos": f(pos), "decay": f(tiles(decay)), "dft": f(tiles(fwd)), "idft": f(tiles(inv)),
            "inv_cnt": f(1.0 / cnt), "ident": f(np.eye(P)), "iota": f(np.tile(np.arange(P), (P, 1)))}


def layouts(a):
    def stationary(w):
        return w.reshape(w.shape[0] // P, P, w.shape[1] // P, P).transpose(2, 1, 0, 3)

    def cols(v):
        return v.reshape(-1, P).T

    w_out = np.concatenate([stationary(a["w_pool_out"][0]), stationary(a["w_hyena_out"][0])], axis=2)
    conv = a["conv_w"][0]
    u = a["peer_u"][0].reshape(P, NK, KD, P)
    out = {
        "x0": a["x_prompt"][0].reshape(LT, P, D).transpose(1, 0, 2), "x1": a["x_sample"][0].reshape(LT, P, D).transpose(1, 0, 2),
        "norm1_g": a["norm1_g"], "norm2_g": a["norm2_g"], "normf_g": a["normf_g"][None],
        "w_in": stationary(a["w_in"][0]).reshape(-1, P, D), "w_out": w_out.reshape(-1, P, D),
        "w_o": a["w_o"][0].reshape(KD, P, D), "wq": stationary(a["peer_wq"][0]).reshape(-1, P, D),
        "pool_w": a["pool_w"][0].transpose(1, 0, 2), "pool_scale": cols(a["pool_scale"][0]),
        "conv_w": conv.reshape(3, -1, P).transpose(2, 0, 1), "conv_b": cols(a["conv_b"][0]),
        "filt_w1": a["filt_w1"][0], "filt_w2": a["filt_w2"][0], "filt_w3": a["filt_w3"][0],
        "filt_vec": np.stack([a["filt_b1"][0], a["filt_f1"][0], a["filt_b2"][0], a["filt_f2"][0]], axis=1),
        "hyena_bias": cols(a["hyena_bias"][0]),
        "keys": a["peer_keys"][0].reshape(2 * H, NK, P).transpose(2, 0, 1),
        "peer_u": u.transpose(1, 3, 2, 0).reshape(NK, P, D),
        "peer_v": a["peer_v"][0].reshape(P, NK, D).transpose(1, 0, 2),
    }
    return {k: np.ascontiguousarray(v) for k, v in out.items()}


SCRATCH = {
    "mixed": (KD, NSEQ, P, L), "h": (P, TT * D), "scores": (TT, H, P, 2 * NK),
    "act": (NK, P, T), "gates": (T // 64, P, NK * 64),
}


def assemble(nc, arrays):
    dram = {n: nc.dram_tensor(f"in_{n}", v.shape, F32, kind="ExternalInput").ap() for n, v in arrays.items()}
    dram["x"] = (dram["x0"], dram["x1"])
    for n, shape in SCRATCH.items():
        dram[n] = nc.dram_tensor(f"tmp_{n}", shape, F32, kind="Internal").ap()
    dram["scores_flat"] = dram["scores"].rearrange("t h p k -> (t h) p k")
    out = [nc.dram_tensor(f"out_{s}", (1, L, D), F32, kind="ExternalOutput").ap().rearrange("a t d -> (a t) d")
           for s in range(NSEQ)]
    program(nc, dram, out)


def kernel(**inputs):
    import concourse.bacc as bacc
    from concourse.bass_utils import run_bass_kernel_spmd

    arrays = {**constants(), **layouts({k: np.asarray(v) for k, v in inputs.items()})}
    nc = bacc.Bacc("TRN2", target_bir_lowering=False, num_devices=1)
    assemble(nc, arrays)
    r = run_bass_kernel_spmd(nc, [{f"in_{n}": v for n, v in arrays.items()}], core_ids=[0])
    return tuple(r.results[0][f"out_{s}"] for s in range(NSEQ))
```

```python
from contextlib import ExitStack

import concourse.bass as bass
import numpy as np
from concourse import mybir

F32 = mybir.dt.float32
F32R = mybir.dt.float32r
U32 = mybir.dt.uint32
ALU = mybir.AluOpType
ACT = mybir.ActivationFunctionType
X = mybir.AxisListType.X

P = 128
D = 1024
KD = D // P
NSEQ = 2
L = 512
T = NSEQ * L
TT = T // P
LT = L // P
C = 512
CT = C // P
WINDOWS = (2, 4, 8, 16)
PAD = 8
N_FFT = 2 * L
H = 8
NK = 128
TOPK = 16
HID = 64
FEMB = 33
EPS = 1e-6
LOWEST = -3.0e38
A_T, X0_T, X1_T, V_T, GA_T, GB_T = 0, 4, 8, 12, 16, 24
TWO_PI = (6.28125, 1.9353071693331003e-3, 1.0253131677018246e-11)
ROUND = 12582912.0
ONE = 1


class Steps:

    def __init__(self, eng, sem, base=0, start=0):
        self.eng, self.sem, self.base, self.start, self.n = eng, sem, base, start, 0

    def did(self, ins):
        ins.then_inc(self.sem, 1)
        self.n += 1
        return ins

    def settle(self):
        self.eng.wait_ge(self.sem, self.start + self.base + self.n)


def f32(ap):
    return ap.bitcast(F32)


class Mem:

    def __init__(self, nc, ctx, side="left"):
        self.nc, self.ctx, self.side, self.sems, self.held = nc, ctx, side, [], []

    def sb(self, name, shape, dt=F32):
        return self.ctx.enter_context(self.nc.sbuf_tensor(name, shape, dt, side=self.side))

    def ps(self, name, shape):
        return self.ctx.enter_context(self.nc.psum_tensor(name, shape, F32))

    def sem(self, name):
        self.held.append(self.nc.semaphore(name))
        self.sems.append(self.held[-1].__enter__())
        return self.sems[-1]

    def release(self):
        with self.nc.Block() as block:
            @block.sync
            def _(sp):
                for sem in self.sems:
                    sp.sem_clear(sem)
        while self.held:
            self.held.pop().__exit__(None, None, None)

    def start_at_one(self, sp):
        for sem in self.sems:
            sp.sem_inc(sem, ONE)


def products(pe, out, w_hi, w_lo, m_hi, m_lo, first, last):
    pe.matmul(out, w_lo, m_hi, start=first, stop=False)
    pe.matmul(out, w_hi, m_lo, start=False, stop=False)
    return pe.matmul(out, w_hi, m_hi, start=False, stop=last)


def filters(nc, dram, K, x_sb, x_in):
    with ExitStack() as ctx:
        m = Mem(nc, ctx)
        ctx.callback(m.release)
        dft = m.sb("dft", [P, LT, N_FFT])
        pos = m.sb("filt_pos", [FEMB, L])
        w1 = m.sb("filt_w1", [FEMB, HID])
        w2 = m.sb("filt_w2", [HID, HID])
        w3 = m.sb("filt_w3", [HID, 2 * C])
        vec = m.sb("filt_vec", [HID, 4])
        decay = m.sb("decay", [P, LT, C])
        h1 = m.sb("h1", [HID, L])
        turns = m.sb("turns", [HID, L])
        h2 = m.sb("h2", [HID, L])
        fwd = m.sb("fwd", [P, LT, C])
        bwd = m.sb("bwd", [P, LT, C])
        even = m.sb("even", [P, LT, C])
        even_hi, even_lo = m.sb("even_hi", [P, LT, C], F32R), m.sb("even_lo", [P, LT, C], F32R)
        odd_hi, odd_lo = m.sb("odd_hi", [P, LT, C], F32R), m.sb("odd_lo", [P, LT, C], F32R)
        net_ps = m.ps("net_ps", [HID, L])
        taps_ps = [m.ps(f"taps_ps{b}", [P, C]) for b in range(2)]
        spec_ps = [m.ps(f"spec_ps{b}", [P, C]) for b in range(2)]
        small_in, dft_in, decay_in = m.sem("small_in"), m.sem("dft_in"), m.sem("decay_in")
        net_done, sin_done = m.sem("net_done"), m.sem("sin_done")
        arg_done, taps_done, taps_read = m.sem("arg_done"), m.sem("taps_done"), m.sem("taps_read")
        hi_done, lo_done = m.sem("fhi_done"), m.sem("flo_done")
        spec_done, spec_read = m.sem("spec_done"), m.sem("spec_read")
        vsteps = m.sem("f_vsteps")
        block = ctx.enter_context(nc.Block())

        @block.sync
        def _(sp):
            for dst, name in ((pos, "filt_pos"), (w1, "filt_w1"), (w2, "filt_w2"), (w3, "filt_w3"), (vec, "filt_vec")):
                sp.dma_start(dst[:], dram[name]).then_inc(small_in, 16)
            sp.dma_start(decay[:], dram["decay"]).then_inc(decay_in, 16)
            sp.dma_start(dft[:], dram["dft"]).then_inc(dft_in, 16)
            for s in range(NSEQ):
                sp.dma_start(x_sb[:, s * LT:(s + 1) * LT], dram["x"][s]).then_inc(x_in[s], 16)

        @block.tensor
        def _(pe):
            pe.wait_ge(small_in, 5 * 16)
            pe.matmul(net_ps[:], w1[:], pos[:], start=True, stop=True).then_inc(net_done, 1)
            pe.wait_ge(sin_done, 1)
            pe.matmul(net_ps[:], w2[:], h1[:], start=True, stop=True).then_inc(net_done, 1)
            pe.wait_ge(sin_done, 2)
            for n in range(2 * LT):
                lt, half = n // 2, n % 2
                if n >= 2:
                    pe.wait_ge(taps_read, n - 1)
                pe.matmul(taps_ps[half][:], h2[:, lt * P:(lt + 1) * P], w3[:, half * C:(half + 1) * C],
                          start=True, stop=True).then_inc(taps_done, 1)
            pe.wait_ge(lo_done, 3)
            for n, (col, hi, lo) in enumerate(
                    [(kt, even_hi, even_lo) for kt in range(4)] + [(kt, odd_hi, odd_lo) for kt in range(4, 8)]
                    + [(4, even_hi, even_lo)]):
                if n >= 2:
                    pe.wait_ge(spec_read, n - 1)
                for c in range(LT):
                    last = products(pe, spec_ps[n % 2][:], K["dft_hi"][:, c, col * P:(col + 1) * P],
                                    K["dft_lo"][:, c, col * P:(col + 1) * P], hi[:, c], lo[:, c], c == 0, c == LT - 1)
                last.then_inc(spec_done, 1)

        @block.scalar
        def _(act):
            act.wait_ge(arg_done, 1)
            act.activation(h1[:], turns[:], ACT.Sin).then_inc(sin_done, 1)
            act.wait_ge(arg_done, 2)
            act.activation(h2[:], turns[:], ACT.Sin).then_inc(sin_done, 1)
            act.wait_ge(dft_in, 16)
            act.activation(K["dft_hi"][:], dft[:], ACT.Copy).then_inc(hi_done, 1)
            act.wait_ge(taps_read, 2 * LT + 1)
            act.activation(even_hi[:], even[:], ACT.Copy).then_inc(hi_done, 1)
            act.wait_ge(taps_read, 2 * LT + 2)
            act.activation(odd_hi[:], fwd[:], ACT.Copy).then_inc(hi_done, 1)

        @block.gpsimd
        def _(pool):
            pool.wait_ge(hi_done, 1)
            pool.tensor_tensor(K["dft_lo"][:], dft[:], f32(K["dft_hi"][:]), ALU.subtract).then_inc(lo_done, 1)

        @block.vector
        def _(dve):
            s = Steps(dve, vsteps)
            dve.wait_ge(small_in, 5 * 16)
            for layer in range(2):
                b, f = vec[:, 2 * layer:2 * layer + 1], vec[:, 2 * layer + 1:2 * layer + 2]
                arg = h2 if layer == 0 else h1
                dve.wait_ge(net_done, layer + 1)
                s.did(dve.tensor_scalar(arg[:], net_ps[:], b, f, ALU.add, ALU.mult))
                s.settle()
                if layer == 1:
                    dve.wait_ge(sin_done, 1)
                s.did(dve.tensor_scalar(turns[:], arg[:], 1.0 / (2 * np.pi), ROUND, ALU.mult, ALU.add))
                s.settle()
                s.did(dve.tensor_scalar(turns[:], turns[:], ROUND, None, ALU.subtract))
                s.settle()
                for part in TWO_PI:
                    s.did(dve.scalar_tensor_tensor(out=arg[:], in0=turns[:], scalar=-part, in1=arg[:],
                                                   op0=ALU.mult, op1=ALU.add))
                    s.settle()
                dve.tensor_scalar(turns[:], arg[:], 3.1415925, -3.1415925, ALU.min, ALU.max).then_inc(arg_done, 1)
            dve.wait_ge(decay_in, 16)
            for n in range(2 * LT):
                dve.wait_ge(taps_done, n + 1)
                dve.tensor_tensor((fwd, bwd)[n % 2][:, n // 2], taps_ps[n % 2][:], decay[:, n // 2],
                                  ALU.mult).then_inc(taps_read, 1)
            dve.wait_ge(taps_read, 2 * LT)
            dve.tensor_tensor(even[:], fwd[:], bwd[:], ALU.add).then_inc(taps_read, 1)
            dve.wait_ge(taps_read, 2 * LT + 1)
            dve.tensor_tensor(fwd[:], fwd[:], bwd[:], ALU.subtract).then_inc(taps_read, 1)
            dve.wait_ge(hi_done, 2)
            dve.tensor_tensor(even_lo[:], even[:], f32(even_hi[:]), ALU.subtract).then_inc(lo_done, 1)
            dve.wait_ge(hi_done, 3)
            dve.tensor_tensor(odd_lo[:], fwd[:], f32(odd_hi[:]), ALU.subtract).then_inc(lo_done, 1)
            for n in range(9):
                dve.wait_ge(spec_done, n + 1)
                if n < 4:
                    dve.tensor_copy(K["k_re"][:, n], spec_ps[n % 2][:]).then_inc(spec_read, 1)
                elif n < 8:
                    dve.tensor_copy(K["k_im"][:, n - 4], spec_ps[n % 2][:]).then_inc(spec_read, 1)
                else:
                    dve.wait_ge(spec_read, 8)
                    s.did(dve.tensor_copy(K["k_re0"][:], K["k_re"][:, 0]))
                    s.settle()
                    dve.tensor_copy(K["k_re0"][0:1, :], spec_ps[n % 2][0:1, :]).then_inc(spec_read, 1)
                    dve.memset(K["k_im"][0:1, 0], 0.0).then_inc(spec_read, 1)


def norm_transpose(nc, dram, tag, src_in, src, gain, keep, x_hi, x_lo):
    with ExitStack() as ctx:
        m = Mem(nc, ctx)
        ctx.callback(m.release)
        gain_sb = m.sb(f"{tag}_gain", [P, D])
        ident = m.sb(f"{tag}_ident", [P, P])
        normed = [m.sb(f"{tag}_normed{b}", [P, D]) for b in range(2)]
        sq = m.sb(f"{tag}_sq", [P, D])
        ss, rstd = m.sb(f"{tag}_ss", [P, TT]), m.sb(f"{tag}_rstd", [P, TT])
        tp = [m.ps(f"{tag}_tp{b}", [P, KD, P]) for b in range(2)]
        const_in, kept = m.sem(f"{tag}_const_in"), m.sem(f"{tag}_kept")
        squared, ms_done, root, inv = (m.sem(f"{tag}_{n}") for n in ("squared", "ms_done", "root", "inv"))
        normed_done, turned = m.sem(f"{tag}_normed_done"), m.sem(f"{tag}_turned")
        hi_done, lo_done = m.sem(f"{tag}_hi_done"), m.sem(f"{tag}_lo_done")
        block = ctx.enter_context(nc.Block())

        @block.sync
        def _(sp):
            sp.dma_start(ident[:], dram["ident"]).then_inc(const_in, 16)
            sp.dma_start(gain_sb[:], dram[gain].broadcast_to([P, D])).then_inc(const_in, 16)
            m.start_at_one(sp)
            if keep is not None:
                sp.dma_start(keep, src[:]).then_inc(kept, 16)
                sp.wait_ge(kept, ONE + 16)

        @block.scalar
        def _(act):
            for tt in range(TT):
                if src_in is not None:
                    act.wait_ge(src_in[tt // LT], 16)
                if tt:
                    act.wait_ge(squared, ONE + tt)
                act.activation(sq[:], src[:, tt], ACT.Square, accum_out=ss[:, tt:tt + 1]).then_inc(squared, 1)
                if tt % LT == LT - 1:
                    s = tt // LT
                    act.wait_ge(ms_done, ONE + s + 1)
                    act.activation(rstd[:, s * LT:(s + 1) * LT], ss[:, s * LT:(s + 1) * LT], ACT.Sqrt).then_inc(root, 1)
            with act.Fori(0, TT // 2) as i:
                for b in range(2):
                    act.wait_ge(turned, ONE + 2 * i + b + 1)
                    act.activation(x_hi[:, :, bass.ts(2 * i + b, P)], tp[b][:], ACT.Copy).then_inc(hi_done, 1)

        @block.vector
        def _(dve):
            def scales(s):
                c = slice(s * LT, (s + 1) * LT)
                dve.wait_ge(squared, ONE + (s + 1) * LT)
                dve.tensor_scalar(ss[:, c], ss[:, c], 1.0 / D, EPS, ALU.mult, ALU.add).then_inc(ms_done, 1)
                dve.wait_ge(root, ONE + s + 1)
                dve.reciprocal(rstd[:, c], rstd[:, c]).then_inc(inv, 1)

            scales(0)
            dve.wait_ge(inv, ONE + 1)
            dve.wait_ge(const_in, ONE + 32)
            if src_in is not None:
                for s in range(NSEQ):
                    dve.wait_ge(src_in[s], 16)

            def normalise(tt, b):
                dve.wait_ge(turned, ONE + tt - b)
                dve.scalar_tensor_tensor(out=normed[b][:], in0=src[:, tt], scalar=rstd[:, bass.ds(tt, 1)],
                                         in1=gain_sb[:], op0=ALU.mult, op1=ALU.mult).then_inc(normed_done, 1)

            def low(tt, b):
                dve.wait_ge(hi_done, ONE + tt + 1)
                dve.tensor_tensor(x_lo[:, :, bass.ts(tt, P)], tp[b][:], f32(x_hi[:, :, bass.ts(tt, P)]),
                                  ALU.subtract).then_inc(lo_done, 1)

            normalise(0, 0)
            normalise(1, 1)
            scales(1)
            dve.wait_ge(inv, ONE + 2)
            with dve.Fori(0, TT // 2 - 1) as i:
                low(2 * i, 0)
                normalise(2 * i + 2, 0)
                low(2 * i + 1, 1)
                normalise(2 * i + 3, 1)
            low(TT - 2, 0)
            low(TT - 1, 1)

        @block.tensor
        def _(pe):
            pe.wait_ge(const_in, ONE + 32)
            with pe.Fori(0, TT // 2) as i:
                for b in range(2):
                    pe.wait_ge(normed_done, ONE + 2 * i + b + 1)
                    if b == 0:
                        pe.wait_ge(lo_done, ONE + 2 * i)
                    for k in range(KD):
                        t = pe.transpose(tp[b][:, k], normed[b][:, k * P:(k + 1) * P], ident[:])
                    t.then_inc(turned, 1)


class Stream:

    def __init__(self, m, tag, slots):
        self.slots = slots
        self.raw = [m.sb(f"{tag}_raw{b}", [P, D]) for b in range(slots)]
        self.hi = [m.sb(f"{tag}_hi{b}", [P, D], F32R) for b in range(slots)]
        self.lo = [m.sb(f"{tag}_lo{b}", [P, D], F32R) for b in range(slots)]
        self.landed = [m.sem(f"{tag}_landed{b}") for b in range(slots)]
        self.hi_done, self.lo_done, self.used = (m.sem(f"{tag}_{n}") for n in ("hi_done", "lo_done", "used"))


def split_first(act, st):
    act.wait_ge(st.landed[0], ONE + 16)
    act.activation(st.hi[0][:], st.raw[0][:], ACT.Copy).then_inc(st.hi_done, 1)


def split_next(act, st, i, b):
    n = 1 - b
    act.wait_ge(st.landed[n], ONE + 16 * (i + b) + 16)
    if b:
        act.wait_ge(st.used, ONE + 2 * i + 1)
    else:
        act.wait_ge(st.used, ONE + 2 * i)
    act.activation(st.hi[n][:], st.raw[n][:], ACT.Copy).then_inc(st.hi_done, 1)


def project_conv(nc, K, b, ps, uc, conv_col, dve, s):
    w = K["conv_w"]
    s.did(dve.scalar_tensor_tensor(out=uc[:, :, 1:L], in0=ps[:, :, 0:L - 1], scalar=w[:, 0, bass.ds(conv_col, 1)],
                                   in1=uc[:, :, 1:L], op0=ALU.mult, op1=ALU.add))
    s.settle()
    return dve.scalar_tensor_tensor(out=uc[:, :, 0:L - 1], in0=ps[:, :, 1:L], scalar=w[:, 2, bass.ds(conv_col, 1)],
                                    in1=uc[:, :, 0:L - 1], op0=ALU.mult, op1=ALU.add)


def gate_product(nc, dram, K, x_hi, x_lo, z_t):
    with ExitStack() as ctx:
        m = Mem(nc, ctx)
        st = Stream(m, "zw", 2)
        uc = [m.sb(f"z_uc{b}", [P, NSEQ, L]) for b in range(2)]
        ps = [m.ps(f"z_ps{b}", [P, NSEQ, L]) for b in range(2)]
        conv_in, mid, read, zdone, vs = (m.sem(f"z_{n}") for n in ("conv_in", "mid", "read", "done", "vs"))
        block = ctx.enter_context(nc.Block())

        @block.sync
        def _(sp):
            m.start_at_one(sp)
            sp.dma_start(K["conv_w"][:], dram["conv_w"]).then_inc(conv_in, 16)
            sp.dma_start(K["conv_b"][:], dram["conv_b"]).then_inc(conv_in, 16)
            with sp.Fori(0, CT) as i:
                for b in range(2):
                    sp.wait_ge(st.lo_done, ONE + 2 * i)
                    sp.dma_start(st.raw[b][:], dram["w_in"][bass.ds(i + (X1_T, V_T)[b], 1)]).then_inc(st.landed[b], 16)

        @block.gpsimd
        def _(pool):
            with pool.Fori(0, CT) as i:
                for b in range(2):
                    pool.wait_ge(st.hi_done, ONE + 2 * i + b + 1)
                    pool.tensor_tensor(st.lo[b][:], st.raw[b][:], f32(st.hi[b][:]), ALU.subtract).then_inc(st.lo_done, 1)

        @block.tensor
        def _(pe):
            with pe.Fori(0, CT) as i:
                for b in range(2):
                    pe.wait_ge(st.lo_done, ONE + 2 * i + b + 1)
                    pe.wait_ge(read, ONE + 2 * i)
                    for k in range(KD):
                        c = slice(k * P, (k + 1) * P)
                        for s in range(NSEQ):
                            t = slice(s * L, (s + 1) * L)
                            last = products(pe, ps[b][:, s], st.hi[b][:, c], st.lo[b][:, c], x_hi[:, k, t],
                                            x_lo[:, k, t], k == 0, k == KD - 1)
                    last.then_inc(st.used, 1)

        @block.scalar
        def _(act):
            act.wait_ge(conv_in, ONE + 32)

            def turn(i, b, ahead):
                if ahead:
                    split_next(act, st, i, b)
                act.wait_ge(st.used, ONE + 2 * i + b + 1)
                act.wait_ge(zdone, ONE + i)
                col = i + (X1_T, V_T)[b] - X0_T
                act.activation(uc[b][:], ps[b][:], ACT.Identity, bias=K["conv_b"][:, bass.ds(col, 1)],
                               scale=K["conv_w"][:, 1, bass.ds(col, 1)]).then_inc(mid, 1)

            split_first(act, st)
            with act.Fori(0, CT - 1) as i:
                for b in range(2):
                    turn(i, b, True)
            turn(CT - 1, 0, True)
            turn(CT - 1, 1, False)

        @block.vector
        def _(dve):
            with dve.Fori(0, CT) as i:
                s = Steps(dve, vs, 2 * i, ONE)
                for b in range(2):
                    dve.wait_ge(mid, ONE + 2 * i + b + 1)
                    project_conv(nc, K, b, ps[b], uc[b], i + (X1_T, V_T)[b] - X0_T, dve, s).then_inc(read, 1)
                dve.wait_ge(read, ONE + 2 * i + 2)
                dve.tensor_tensor(z_t[:, i], uc[0][:].rearrange("p s t -> p (s t)"),
                                  uc[1][:].rearrange("p s t -> p (s t)"), ALU.mult).then_inc(zdone, 1)


def forward_dft(nc, dram, K, z_t, y_spec):
    with ExitStack() as ctx:
        m = Mem(nc, ctx)
        ident = m.sb("fd_ident", [P, P])
        z_hi, z_lo = m.sb("z_hi", [P, TT, C], F32R), m.sb("z_lo", [P, TT, C], F32R)
        prod = [m.sb(f"fd_prod{n}", [P, C]) for n in range(4)]
        tp = [m.ps(f"fd_tp{b}", [P, CT, P]) for b in range(2)]
        re = [m.ps(f"fd_re{b}", [P, C]) for b in range(2)]
        im = [m.ps(f"fd_im{b}", [P, C]) for b in range(2)]
        ident_in, turned, hi_done, lo_done = (m.sem(f"fd_{n}") for n in ("ident_in", "turned", "hi", "lo"))
        spec, mult, summed = (m.sem(f"fd_{n}") for n in ("spec", "mult", "summed"))
        block = ctx.enter_context(nc.Block())
        jobs = [(s, kt) for s in range(NSEQ) for kt in range(4)]

        @block.sync
        def _(sp):
            m.start_at_one(sp)
            sp.dma_start(ident[:], dram["ident"]).then_inc(ident_in, 16)

        @block.tensor
        def _(pe):
            pe.wait_ge(ident_in, ONE + 16)
            for tt in range(TT):
                if tt >= 2:
                    pe.wait_ge(lo_done, ONE + tt - 1)
                for c in range(CT):
                    t = pe.transpose(tp[tt % 2][:, c], z_t[:, c, tt * P:(tt + 1) * P], ident[:])
                t.then_inc(turned, 1)
            for n, (s, kt) in enumerate(jobs):
                pe.wait_ge(lo_done, ONE + LT * (s + 1))
                if n >= 2:
                    pe.wait_ge(mult, ONE + n - 1)
                for half, out in ((0, re), (1, im)):
                    col = slice((4 * half + kt) * P, (4 * half + kt + 1) * P)
                    for c in range(LT):
                        last = products(pe, out[n % 2][:], K["dft_hi"][:, c, col], K["dft_lo"][:, c, col],
                                        z_hi[:, s * LT + c], z_lo[:, s * LT + c], c == 0, c == LT - 1)
                last.then_inc(spec, 1)

        @block.scalar
        def _(act):
            for tt in range(TT):
                act.wait_ge(turned, ONE + tt + 1)
                act.activation(z_hi[:, tt], tp[tt % 2][:], ACT.Copy).then_inc(hi_done, 1)

        @block.vector
        def _(dve):
            for tt in range(TT):
                dve.wait_ge(hi_done, ONE + tt + 1)
                dve.tensor_tensor(z_lo[:, tt], tp[tt % 2][:], f32(z_hi[:, tt]), ALU.subtract).then_inc(lo_done, 1)
            for n, (s, kt) in enumerate(jobs):
                k_re, k_im = K["k_re"][:, kt], K["k_im"][:, kt]
                k_re_im = K["k_re0"][:] if kt == 0 else k_re
                dve.wait_ge(spec, ONE + n + 1)
                if n:
                    dve.wait_ge(summed, ONE + 2 * n)
                dve.tensor_tensor(prod[0][:], re[n % 2][:], k_re, ALU.mult)
                dve.tensor_tensor(prod[1][:], im[n % 2][:], k_im, ALU.mult)
                dve.tensor_tensor(prod[2][:], re[n % 2][:], k_im, ALU.mult)
                dve.tensor_tensor(prod[3][:], im[n % 2][:], k_re_im, ALU.mult).then_inc(mult, 1)

        @block.gpsimd
        def _(pool):
            for n, (s, kt) in enumerate(jobs):
                pool.wait_ge(mult, ONE + n + 1)
                pool.tensor_tensor(y_spec[:, kt, s], prod[0][:], prod[1][:], ALU.subtract).then_inc(summed, 1)
                pool.tensor_tensor(y_spec[:, 4 + kt, s], prod[2][:], prod[3][:], ALU.add).then_inc(summed, 1)


def inverse_dft(nc, dram, y_spec, z_t):
    with ExitStack() as ctx:
        m = Mem(nc, ctx)
        idft = m.sb("idft", [P, 8, L])
        g_hi, g_lo = m.sb("idft_hi", [P, 8, L], F32R), m.sb("idft_lo", [P, 8, L], F32R)
        y_hi, y_lo = m.sb("ys_hi", [P, 8, C], F32R), m.sb("ys_lo", [P, 8, C], F32R)
        bias = m.sb("hy_bias", [P, CT])
        ps = [m.ps(f"id_ps{b}", [P, L]) for b in range(4)]
        idft_in = [m.sem(f"id_in{n}") for n in range(2)]
        bias_in, hi_done, lo_done, g_hi_done, g_lo_done, inv, read = (
            m.sem(f"id_{n}") for n in ("bias_in", "hi", "lo", "g_hi", "g_lo", "inv", "read"))
        block = ctx.enter_context(nc.Block())

        @block.sync
        def _(sp):
            m.start_at_one(sp)
            for n in range(2):
                sp.dma_start(idft[:, 4 * n:4 * n + 4], dram["idft"][:, 4 * n:4 * n + 4]).then_inc(idft_in[n], 16)
            sp.dma_start(bias[:], dram["hyena_bias"]).then_inc(bias_in, 16)

        @block.scalar
        def _(act):
            for k in range(8):
                act.activation(y_hi[:, k], y_spec[:, k, 0], ACT.Copy).then_inc(hi_done, 1)
                act.wait_ge(idft_in[k // 4], ONE + 16)
                act.activation(g_hi[:, k], idft[:, k], ACT.Copy).then_inc(g_hi_done, 1)
            for k in range(8):
                if k == 0:
                    act.wait_ge(inv, ONE + CT)
                act.activation(y_hi[:, k], y_spec[:, k, 1], ACT.Copy).then_inc(hi_done, 1)

        @block.gpsimd
        def _(pool):
            for k in range(8):
                pool.wait_ge(g_hi_done, ONE + k + 1)
                pool.tensor_tensor(g_lo[:, k], idft[:, k], f32(g_hi[:, k]), ALU.subtract).then_inc(g_lo_done, 1)

        @block.vector
        def _(dve):
            def low(s):
                for k in range(8):
                    dve.wait_ge(hi_done, ONE + 8 * s + k + 1)
                    dve.tensor_tensor(y_lo[:, k], y_spec[:, k, s], f32(y_hi[:, k]), ALU.subtract).then_inc(lo_done, 1)

            def add(s, c):
                n = CT * s + c
                dve.wait_ge(inv, ONE + n + 1)
                z = z_t[:, c, s * L:(s + 1) * L]
                dve.scalar_tensor_tensor(out=z, in0=z, scalar=bias[:, c:c + 1], in1=ps[n % 4][:],
                                         op0=ALU.mult, op1=ALU.add).then_inc(read, 1)

            low(0)
            dve.wait_ge(bias_in, ONE + 16)
            for c in range(CT - 1):
                add(0, c)
            low(1)
            add(0, CT - 1)
            for c in range(CT):
                add(1, c)

        @block.tensor
        def _(pe):
            for k in range(8):
                pe.wait_ge(lo_done, ONE + k + 1)
                pe.wait_ge(g_lo_done, ONE + k + 1)
                for c in range(CT):
                    last = products(pe, ps[c][:], y_hi[:, k, c * P:(c + 1) * P], y_lo[:, k, c * P:(c + 1) * P],
                                    g_hi[:, k], g_lo[:, k], k == 0, k == 7)
                    if k == 7:
                        last.then_inc(inv, 1)
            for c in range(CT):
                pe.wait_ge(lo_done, ONE + 16)
                pe.wait_ge(read, ONE + c + 1)
                for k in range(8):
                    last = products(pe, ps[c][:], y_hi[:, k, c * P:(c + 1) * P], y_lo[:, k, c * P:(c + 1) * P],
                                    g_hi[:, k], g_lo[:, k], k == 0, k == 7)
                last.then_inc(inv, 1)


def branches(nc, dram, K, x_hi, x_lo, y_t, br_hi, br_lo):
    with ExitStack() as ctx:
        m = Mem(nc, ctx)
        st = Stream(m, "bw", 2)
        uc = m.sb("b_uc", [P, NSEQ, L])
        W = L + 2 * PAD
        a_pad = m.sb("a_pad", [P, NSEQ, W])
        sums = [m.sb(f"pool_sum{n}", [P, NSEQ, W]) for n in range(2)]
        inv_cnt = m.sb("inv_cnt", [P, L])
        pooled = m.sb("pooled", [P, NSEQ, L])
        pool_w = m.sb("pool_w_sb", [P, CT, P])
        pool_scale = m.sb("pool_scale_sb", [P, CT])
        ps = [m.ps(f"b_ps{b}", [P, NSEQ, L]) for b in range(2)]
        mix = m.ps("mix_ps", [P, NSEQ, L])
        const_in, cnt_in, mid, read, vs, a_in, yb, ybhi = (m.sem(f"b_{n}") for n in (
            "const_in", "cnt_in", "mid", "read", "vs", "a_in", "yb", "ybhi"))
        pooled_done, mixed, mix_hi, mix_lo, zeroed, yblo = (m.sem(f"b_{n}") for n in (
            "pooled", "mixed", "mix_hi", "mix_lo", "zeroed", "yblo"))
        block = ctx.enter_context(nc.Block())

        @block.sync
        def _(sp):
            m.start_at_one(sp)
            sp.dma_start(pool_w[:], dram["pool_w"]).then_inc(const_in, 16)
            sp.dma_start(pool_scale[:], dram["pool_scale"]).then_inc(const_in, 16)
            for j in range(CT):
                for b in range(2):
                    if j:
                        sp.wait_ge(st.lo_done, ONE + 2 * j - 1 + b)
                    sp.dma_start(st.raw[b][:], dram["w_in"][(X0_T, A_T)[b] + j]).then_inc(st.landed[b], 16)
                if j:
                    sp.wait_ge(pooled_done, ONE + j)
                sp.dma_start(inv_cnt[:], dram["inv_cnt"][j:j + 1].broadcast_to([P, L])).then_inc(cnt_in, 16)

        @block.tensor
        def _(pe):
            pe.wait_ge(const_in, ONE + 32)

            def mix_group(g):
                pe.wait_ge(pooled_done, ONE + g + 1)
                if g:
                    pe.wait_ge(mix_lo, ONE + g)
                for s in range(NSEQ):
                    last = pe.matmul(mix[:, s], pool_w[:, g], pooled[:, s], start=True, stop=True)
                last.then_inc(mixed, 1)

            for j in range(CT):
                for b in range(2):
                    pe.wait_ge(st.lo_done, ONE + 2 * j + b + 1)
                    if j:
                        pe.wait_ge((read, a_in)[b], ONE + j)
                    for k in range(KD):
                        c = slice(k * P, (k + 1) * P)
                        for s in range(NSEQ):
                            t = slice(s * L, (s + 1) * L)
                            last = products(pe, ps[b][:, s], st.hi[b][:, c], st.lo[b][:, c], x_hi[:, k, t],
                                            x_lo[:, k, t], k == 0, k == KD - 1)
                    last.then_inc(st.used, 1)
                    if b == 0 and j:
                        mix_group(j - 1)
            mix_group(CT - 1)

        @block.scalar
        def _(act):
            act.wait_ge(const_in, ONE + 32)
            act.wait_ge(zeroed, ONE + 1)

            def after(j):
                col = j
                act.wait_ge(st.used, ONE + 2 * j + 1)
                if j:
                    act.wait_ge(yb, ONE + j)
                act.activation(uc[:], ps[0][:], ACT.Identity, bias=K["conv_b"][:, col:col + 1],
                               scale=K["conv_w"][:, 1, col:col + 1]).then_inc(mid, 1)
                act.wait_ge(st.used, ONE + 2 * j + 2)
                if j:
                    act.wait_ge(pooled_done, ONE + j)
                act.activation(a_pad[:, :, PAD:PAD + L], ps[1][:], ACT.Copy).then_inc(a_in, 1)
                act.wait_ge(yb, ONE + j + 1)
                act.activation(br_hi[:, CT + j], y_t[:, j], ACT.Copy).then_inc(ybhi, 1)
                act.wait_ge(mixed, ONE + j + 1)
                act.activation(br_hi[:, j].rearrange("p (s t) -> p s t", s=NSEQ), mix[:], ACT.Copy,
                               scale=pool_scale[:, j:j + 1]).then_inc(mix_hi, 1)

            def split(n):
                b = n % 2
                act.wait_ge(st.landed[b], ONE + 16 * (n // 2) + 16)
                if n >= 2:
                    act.wait_ge(st.used, ONE + n - 1)
                act.activation(st.hi[b][:], st.raw[b][:], ACT.Copy).then_inc(st.hi_done, 1)

            split(0)
            split(1)
            for j in range(CT):
                if j + 1 < CT:
                    split(2 * j + 2)
                    split(2 * j + 3)
                after(j)

        @block.gpsimd
        def _(pool):
            pool.memset(a_pad[:], 0.0).then_inc(zeroed, 1)

            def split(n):
                b = n % 2
                pool.wait_ge(st.hi_done, ONE + n + 1)
                pool.tensor_tensor(st.lo[b][:], st.raw[b][:], f32(st.hi[b][:]), ALU.subtract).then_inc(st.lo_done, 1)

            split(0)
            split(1)
            for j in range(CT):
                if j + 1 < CT:
                    split(2 * j + 2)
                    split(2 * j + 3)
                pool.wait_ge(ybhi, ONE + j + 1)
                pool.tensor_tensor(br_lo[:, CT + j], y_t[:, j], f32(br_hi[:, CT + j]), ALU.subtract).then_inc(yblo, 1)

        @block.vector
        def _(dve):
            s = Steps(dve, vs, 0, ONE)
            dve.wait_ge(const_in, ONE + 32)
            for j, w in enumerate(WINDOWS):
                dve.wait_ge(mid, ONE + j + 1)
                project_conv(nc, K, 0, ps[0], uc, j, dve, s).then_inc(read, 1)
                dve.wait_ge(read, ONE + j + 1)
                dve.tensor_tensor(y_t[:, j], y_t[:, j], uc[:].rearrange("p s t -> p (s t)"), ALU.mult).then_inc(yb, 1)
                dve.wait_ge(a_in, ONE + j + 1)
                src, width, n = a_pad, 1, 0
                while width < w:
                    span = W - 2 * width + 1
                    s.did(dve.tensor_tensor(sums[n][:, :, 0:span], src[:, :, 0:span], src[:, :, width:width + span],
                                            ALU.add))
                    s.settle()
                    src, width, n = sums[n], 2 * width, 1 - n
                dve.wait_ge(cnt_in, ONE + 16 * (j + 1))
                win = src[:, :, PAD - w // 2:PAD - w // 2 + L]
                if j:
                    dve.wait_ge(mixed, ONE + j)
                for q in range(NSEQ):
                    s.did(dve.tensor_tensor(pooled[:, q], win[:, q], inv_cnt[:], ALU.mult))
                s.settle()
                dve.tensor_tensor(pooled[:], pooled[:], a_pad[:, :, PAD:PAD + L], ALU.subtract).then_inc(pooled_done, 1)
                dve.wait_ge(mix_hi, ONE + j + 1)
                dve.scalar_tensor_tensor(out=br_lo[:, j].rearrange("p (s t) -> p s t", s=NSEQ), in0=mix[:],
                                         scalar=pool_scale[:, j:j + 1],
                                         in1=f32(br_hi[:, j].rearrange("p (s t) -> p s t", s=NSEQ)),
                                         op0=ALU.mult, op1=ALU.subtract).then_inc(mix_lo, 1)


def gated_mix(nc, dram, x_hi, x_lo, br_hi, br_lo):
    with ExitStack() as ctx:
        m = Mem(nc, ctx)
        st = Stream(m, "gw", 3)
        sig = [m.sb(f"sig{b}", [P, NSEQ, L]) for b in range(2)]
        ps = [m.ps(f"g_ps{n}", [P, NSEQ, L]) for n in range(4)]
        mix = m.sb("mix_sb", [P, NSEQ, L])
        sig_done, prod_done, vs, stored = m.sem("g_sig"), m.sem("g_prod"), m.sem("g_vs"), m.sem("g_stored")
        block = ctx.enter_context(nc.Block())

        @block.sync
        def _(sp):
            m.start_at_one(sp)
            with sp.Fori(0, KD) as i:
                for b in range(3):
                    sp.wait_ge(st.lo_done, ONE + 3 * i)
                    src = dram["w_in"][bass.ds(i + (GA_T, GB_T)[b], 1)] if b < 2 else dram["w_out"][bass.ds(i, 1)]
                    sp.dma_start(st.raw[b][:], src).then_inc(st.landed[b], 16)

        @block.gpsimd
        def _(pool):
            with pool.Fori(0, KD) as i:
                for b in range(3):
                    pool.wait_ge(st.hi_done, ONE + 3 * i + b + 1)
                    pool.tensor_tensor(st.lo[b][:], st.raw[b][:], f32(st.hi[b][:]), ALU.subtract).then_inc(st.lo_done, 1)

        @block.tensor
        def _(pe):
            with pe.Fori(0, KD) as i:
                for b in range(3):
                    pe.wait_ge(st.lo_done, ONE + 3 * i + b + 1)
                    if b == 0:
                        pe.wait_ge(sig_done, ONE + 2 * i)
                    if b == 2:
                        pe.wait_ge(prod_done, ONE + i)
                    for k in range(KD):
                        c = slice(k * P, (k + 1) * P)
                        for s in range(NSEQ):
                            t = slice(s * L, (s + 1) * L)
                            if b < 2:
                                out, m_hi, m_lo, first, end = ps[b], x_hi, x_lo, k == 0, k == KD - 1
                            else:
                                out, m_hi, m_lo = ps[2 + k // CT], br_hi, br_lo
                                first, end = k % CT == 0, k % CT == CT - 1
                            last = products(pe, out[:, s], st.hi[b][:, c], st.lo[b][:, c], m_hi[:, k, t],
                                            m_lo[:, k, t], first, end)
                    last.then_inc(st.used, 1)

        @block.scalar
        def _(act):
            def split(i, b):
                act.wait_ge(st.landed[b], ONE + 16 * i + 16)
                act.activation(st.hi[b][:], st.raw[b][:], ACT.Copy).then_inc(st.hi_done, 1)

            def store(i):
                act.wait_ge(prod_done, ONE + i + 1)
                act.dma_start(dram["mixed"][bass.ds(i, 1)].rearrange("n s p t -> p (n s) t"),
                              mix[:]).then_inc(stored, 16)

            def turn(i, first, ahead):
                for b in range(3):
                    if b == 1 and not first:
                        store(i - 1)
                    if b == 0 or ahead:
                        act.wait_ge(st.used, ONE + 3 * i + b)
                        split(i + (b + 2) // 3, (b + 2) % 3)
                    if b < 2:
                        act.wait_ge(st.used, ONE + 3 * i + b + 1)
                        act.wait_ge(prod_done, ONE + i)
                        act.activation(sig[b][:], ps[b][:], ACT.Sigmoid).then_inc(sig_done, 1)

            split(0, 0)
            split(0, 1)
            turn(0, True, True)
            with act.Fori(1, KD - 1) as i:
                turn(i, False, True)
            turn(KD - 1, False, False)
            store(KD - 1)
            act.wait_ge(stored, ONE + 16 * KD)

        @block.vector
        def _(dve):
            with dve.Fori(0, KD) as i:
                s = Steps(dve, vs, 2 * i, ONE)
                dve.wait_ge(st.used, ONE + 3 * i + 3)
                for b in range(2):
                    dve.wait_ge(sig_done, ONE + 2 * i + b + 1)
                    s.did(dve.tensor_tensor(sig[b][:], sig[b][:], ps[2 + b][:], ALU.mult))
                s.settle()
                dve.wait_ge(stored, ONE + 16 * i)
                dve.tensor_tensor(mix[:], sig[0][:], sig[1][:], ALU.add).then_inc(prod_done, 1)


def residual(nc, dram, h):
    S = 4
    with ExitStack() as ctx:
        m = Mem(nc, ctx)
        st = Stream(m, "ow", S)
        m_raw = [m.sb(f"m_raw{b}", [P, L]) for b in range(S)]
        m_in = [m.sem(f"m_in{b}") for b in range(S)]
        m_hi = [m.sb(f"m_hi{b}", [P, L], F32R) for b in range(S)]
        m_lo = [m.sb(f"m_lo{b}", [P, L], F32R) for b in range(S)]
        ps = [[m.ps(f"h_ps{t}_{n}", [P, 512]) for n in range(2)] for t in range(LT)]
        x_in, mhi, mlo, added = (m.sem(f"h_{n}") for n in ("x_in", "mhi", "mlo", "added"))
        block = ctx.enter_context(nc.Block())
        tiles = [(n, n // KD, n % KD, n % S) for n in range(NSEQ * KD)]

        @block.sync
        def _(sp):
            m.start_at_one(sp)
            for n, s, k, b in tiles:
                if n >= S:
                    sp.wait_ge(st.lo_done, ONE + n - S + 1)
                    sp.wait_ge(mlo, ONE + n - S + 1)
                sp.dma_start(st.raw[b][:], dram["w_o"][k]).then_inc(st.landed[b], 16)
                sp.dma_start(m_raw[b][:], dram["mixed"][k, s]).then_inc(m_in[b], 16)
                if k == S - 1:
                    sp.dma_start(h[:, s * LT:(s + 1) * LT], dram["x"][s]).then_inc(x_in, 16)

        @block.scalar
        def _(act):
            for n, s, k, b in tiles:
                act.wait_ge(st.landed[b], ONE + 16 * (n // S + 1))
                if n >= S:
                    act.wait_ge(st.used, ONE + n - S + 1)
                act.activation(st.hi[b][:], st.raw[b][:], ACT.Copy).then_inc(st.hi_done, 1)
                act.wait_ge(m_in[b], ONE + 16 * (n // S + 1))
                act.activation(m_hi[b][:], m_raw[b][:], ACT.Copy).then_inc(mhi, 1)

        @block.gpsimd
        def _(pool):
            for n, s, k, b in tiles:
                pool.wait_ge(st.hi_done, ONE + n + 1)
                pool.tensor_tensor(st.lo[b][:], st.raw[b][:], f32(st.hi[b][:]), ALU.subtract).then_inc(st.lo_done, 1)

        @block.vector
        def _(dve):
            def low(n, b):
                dve.wait_ge(mhi, ONE + n + 1)
                dve.tensor_tensor(m_lo[b][:], m_raw[b][:], f32(m_hi[b][:]), ALU.subtract).then_inc(mlo, 1)

            def add(s):
                dve.wait_ge(x_in, ONE + 16 * (s + 1))
                for t in range(LT):
                    for n in range(2):
                        part = h[:, s * LT + t, n * 512:(n + 1) * 512]
                        dve.tensor_tensor(part, part, ps[t][n][:], ALU.add).then_inc(added, 1)

            for n, s, k, b in tiles:
                if n == KD + S - 1:
                    dve.wait_ge(st.used, ONE + KD)
                    add(0)
                low(n, b)
            dve.wait_ge(st.used, ONE + NSEQ * KD)
            add(1)

        @block.tensor
        def _(pe):
            for n, s, k, b in tiles:
                pe.wait_ge(st.lo_done, ONE + n + 1)
                pe.wait_ge(mlo, ONE + n + 1)
                for t in range(LT):
                    if k == 0 and s:
                        pe.wait_ge(added, ONE + 2 * t + 2)
                    for half in range(2):
                        c, w = slice(half * 512, (half + 1) * 512), slice(t * P, (t + 1) * P)
                        last = products(pe, ps[t][half][:], m_hi[b][:, w], m_lo[b][:, w], st.hi[b][:, c],
                                        st.lo[b][:, c], k == 0, k == KD - 1)
                last.then_inc(st.used, 1)


class Routing:
    STEPS = 34

    def __init__(self, m):
        self.sems = Mem(m.nc, m.ctx)
        self.carrier = m.sb("carrier", [P, 2])
        self.iota = m.sb("iota", [P, P])
        self.rest = [m.sb(f"rest{p}", [P, NK]) for p in range(2)]
        self.top = m.sb("top", [P, 2, TOPK])
        self.top_at = m.sb("top_at", [P, 2, TOPK], U32)
        self.top_key = m.sb("top_key", [P, 2, TOPK])
        self.pairs = m.sb("pairs", [P, TOPK, TOPK])
        self.pairs_rest = m.sb("pairs_rest", [P, TOPK * TOPK])
        self.best = m.sb("best", [P, TOPK])
        self.best_at = m.sb("best_at", [P, TOPK], U32)
        self.rank_u = m.sb("rank_u", [P, 2, TOPK], U32)
        self.rank = m.sb("rank", [P, 2, TOPK])
        self.pick = [m.sb(f"pick{p}", [P, TOPK, TOPK]) for p in range(2)]
        self.sel = m.sb("sel", [P, 3, P])
        self.routed, self.steps = self.sems.sem("routed"), self.sems.sem("route_steps")


def carry_wait(R, dve, at=0):
    return dve.tensor_copy(R.carrier[:, at:at + 1], R.iota[:, 0:1])

def route(R, dve, scores, h, base):
    s = Steps(dve, R.steps, base, ONE)
    out = bass.ds(h * TOPK, TOPK)
    s.did(carry_wait(R, dve))
    for p in range(2):
        s.did(dve.max(R.top[:, p, 0:8], scores[:, p]))
    s.settle()
    s.did(carry_wait(R, dve))
    for p in range(2):
        s.did(dve.match_replace(R.rest[p][:], R.top[:, p, 0:8], scores[:, p], LOWEST))
        s.did(dve.max_index(R.top_at[:, p, 0:8], R.top[:, p, 0:8], scores[:, p]))
    s.settle()
    s.did(carry_wait(R, dve))
    for p in range(2):
        s.did(dve.max(R.top[:, p, 8:16], R.rest[p][:]))
    s.settle()
    s.did(carry_wait(R, dve))
    for p in range(2):
        s.did(dve.max_index(R.top_at[:, p, 8:16], R.top[:, p, 8:16], R.rest[p][:]))
    s.did(dve.tensor_tensor(R.pairs[:], R.top[:, 0].unsqueeze(2).broadcast_to([P, TOPK, TOPK]),
                            R.top[:, 1].unsqueeze(1).broadcast_to([P, TOPK, TOPK]), ALU.add))
    s.settle()
    flat = R.pairs[:].rearrange("p a b -> p (a b)")
    s.did(dve.tensor_copy(R.top_key[:], R.top_at[:]))
    s.did(dve.max(R.best[:, 0:8], flat))
    s.settle()
    s.did(carry_wait(R, dve))
    s.did(dve.match_replace(R.pairs_rest[:], R.best[:, 0:8], flat, LOWEST))
    s.did(dve.max_index(R.best_at[:, 0:8], R.best[:, 0:8], flat))
    s.settle()
    s.did(carry_wait(R, dve))
    s.did(dve.max(R.best[:, 8:16], R.pairs_rest[:]))
    s.settle()
    s.did(carry_wait(R, dve))
    s.did(dve.max_index(R.best_at[:, 8:16], R.best[:, 8:16], R.pairs_rest[:]))
    s.settle()
    s.did(dve.tensor_scalar(R.rank_u[:, 0], R.best_at[:], 4, None, ALU.logical_shift_right))
    s.did(dve.tensor_scalar(R.rank_u[:, 1], R.best_at[:], TOPK - 1, None, ALU.bitwise_and))
    s.did(dve.tensor_scalar(R.sel[:, 2, out], R.best[:], R.best[:, 0:1], None, ALU.subtract))
    s.settle()
    s.did(dve.tensor_copy(R.rank[:], R.rank_u[:]))
    s.settle()
    for p in range(2):
        s.did(dve.tensor_tensor(R.pick[p][:], R.rank[:, p].unsqueeze(2).broadcast_to([P, TOPK, TOPK]),
                                R.iota[:, 0:TOPK].unsqueeze(1).broadcast_to([P, TOPK, TOPK]), ALU.is_equal))
    s.settle()
    for p in range(2):
        s.did(dve.tensor_tensor(R.pick[p][:], R.pick[p][:],
                                R.top_key[:, p].unsqueeze(1).broadcast_to([P, TOPK, TOPK]), ALU.mult))
    s.settle()
    s.did(dve.tensor_reduce(R.sel[:, 0, out], R.pick[0][:], X, ALU.add))
    s.did(dve.tensor_reduce(R.sel[:, 1, out], R.pick[1][:], X, ALU.add))
    assert s.n == Routing.STEPS, s.n
    s.settle()
    dve.sem_inc(R.routed, 1)


def key_scores(nc, dram, R, x_hi, x_lo):
    with ExitStack() as ctx:
        m = Mem(nc, ctx)
        st = Stream(m, "qw", 2)
        keys = m.sb("keys", [P, 2 * H, NK])
        k_hi, k_lo = m.sb("keys_hi", [P, 2 * H, NK], F32R), m.sb("keys_lo", [P, 2 * H, NK], F32R)
        q_hi = [m.sb(f"q_hi{b}", [P, T], F32R) for b in range(2)]
        q_lo = [m.sb(f"q_lo{b}", [P, T], F32R) for b in range(2)]
        sc = m.sb("head_scores", [P, TT, 2, NK])
        q_ps = [m.ps(f"q_ps{b}", [P, NSEQ, L]) for b in range(2)]
        s_ps = [m.ps(f"s_ps{b}", [P, TT, NK]) for b in range(2)]
        keys_in, iota_in, keys_hi_done, keys_lo_done, qhi, qlo, scored, read, stored = (m.sem(f"q_{n}") for n in (
            "keys_in", "iota_in", "keys_hi", "keys_lo", "hi", "lo", "scored", "read", "stored"))
        block = ctx.enter_context(nc.Block())

        @block.sync
        def _(sp):
            m.start_at_one(sp)
            R.sems.start_at_one(sp)
            sp.dma_start(keys[:], dram["keys"]).then_inc(keys_in, 16)
            sp.dma_start(R.iota[:], dram["iota"]).then_inc(iota_in, 16)
            with sp.Fori(0, H) as i:
                for b in range(2):
                    sp.wait_ge(st.lo_done, ONE + 2 * i)
                    sp.dma_start(st.raw[b][:], dram["wq"][bass.ds(2 * i + b, 1)]).then_inc(st.landed[b], 16)

        @block.gpsimd
        def _(pool):
            with pool.Fori(0, H) as i:
                for b in range(2):
                    pool.wait_ge(st.hi_done, ONE + 2 * i + b + 1)
                    pool.tensor_tensor(st.lo[b][:], st.raw[b][:], f32(st.hi[b][:]), ALU.subtract).then_inc(st.lo_done, 1)

        @block.scalar
        def _(act):
            def store(i):
                act.wait_ge(read, ONE + 2 * i + 2)
                act.dma_start(dram["scores"][:, bass.ds(i, 1)].rearrange("n h p k -> p (n h) k"),
                              sc[:].rearrange("p n h k -> p n (h k)")).then_inc(stored, 16)

            def turn(i, b, ahead, earlier):
                if ahead:
                    split_next(act, st, i, b)
                if b and earlier:
                    store(i - 1)
                act.wait_ge(st.used, ONE + 2 * i + b + 1)
                act.wait_ge(scored, ONE + 2 * i)
                act.activation(q_hi[b][:], q_ps[b][:].rearrange("p s t -> p (s t)"), ACT.Copy).then_inc(qhi, 1)

            act.wait_ge(keys_in, ONE + 16)
            act.activation(k_hi[:], keys[:], ACT.Copy).then_inc(keys_hi_done, 1)
            split_first(act, st)
            turn(0, 0, True, False)
            turn(0, 1, True, False)
            with act.Fori(1, H - 1) as i:
                for b in range(2):
                    turn(i, b, True, True)
            turn(H - 1, 0, True, True)
            turn(H - 1, 1, False, True)
            store(H - 1)
            act.wait_ge(stored, ONE + 16 * H)

        @block.vector
        def _(dve):
            def low(i, b):
                dve.wait_ge(qhi, ONE + 2 * i + b + 1)
                dve.tensor_tensor(q_lo[b][:], q_ps[b][:].rearrange("p s t -> p (s t)"), f32(q_hi[b][:]),
                                  ALU.subtract).then_inc(qlo, 1)

            def collect(i, b):
                dve.wait_ge(scored, ONE + 2 * i + b + 1)
                dve.wait_ge(stored, ONE + 16 * i)
                dve.tensor_copy(sc[:, :, b], s_ps[b][:]).then_inc(read, 1)

            def route_head(i):
                dve.wait_ge(read, ONE + 2 * i + 2)
                route(R, dve, sc[:, 0], i, i * Routing.STEPS)

            dve.wait_ge(keys_hi_done, ONE + 1)
            dve.tensor_tensor(k_lo[:], keys[:], f32(k_hi[:]), ALU.subtract).then_inc(keys_lo_done, 1)
            dve.wait_ge(iota_in, ONE + 16)
            low(0, 0)
            low(0, 1)
            collect(0, 0)
            with dve.Fori(1, H) as i:
                low(i, 0)
                collect(i - 1, 1)
                route_head(i - 1)
                low(i, 1)
                collect(i, 0)
            collect(H - 1, 1)
            route_head(H - 1)

        @block.tensor
        def _(pe):
            def queries(i, b):
                pe.wait_ge(st.lo_done, ONE + 2 * i + b + 1)
                for k in range(KD):
                    c = slice(k * P, (k + 1) * P)
                    for s in range(NSEQ):
                        t = slice(s * L, (s + 1) * L)
                        last = products(pe, q_ps[b][:, s], st.hi[b][:, c], st.lo[b][:, c], x_hi[:, k, t],
                                        x_lo[:, k, t], k == 0, k == KD - 1)
                last.then_inc(st.used, 1)

            def scores(i, b, again):
                pe.wait_ge(qlo, ONE + 2 * i + b + 1)
                if again:
                    pe.wait_ge(read, ONE + 2 * i - 1 + b)
                for t in range(TT):
                    c = slice(t * P, (t + 1) * P)
                    hp = bass.ds(2 * i + b, 1)
                    last = products(pe, s_ps[b][:, t], q_hi[b][:, c], q_lo[b][:, c],
                                    k_hi[:, hp].rearrange("p h k -> p (h k)"),
                                    k_lo[:, hp].rearrange("p h k -> p (h k)"), True, True)
                last.then_inc(scored, 1)

            pe.wait_ge(keys_lo_done, ONE + 1)
            queries(0, 0)
            queries(0, 1)
            scores(0, 0, False)
            pe.wait_ge(qlo, ONE + 1)
            queries(1, 0)
            scores(0, 1, False)
            pe.wait_ge(qlo, ONE + 2)
            queries(1, 1)
            scores(1, 0, True)
            with pe.Fori(2, H) as i:
                pe.wait_ge(qlo, ONE + 2 * i - 1)
                queries(i, 0)
                scores(i - 1, 1, True)
                pe.wait_ge(qlo, ONE + 2 * i)
                queries(i, 1)
                scores(i, 0, True)
            scores(H - 1, 1, True)


def experts_in(nc, dram, R, x_hi, x_lo):
    with ExitStack() as ctx:
        m = Mem(nc, ctx)
        st = Stream(m, "uw", 2)
        gel = [m.sb(f"gel{b}", [P, T]) for b in range(2)]
        sc = [m.sb(f"sc{b}", [P, 2, NK]) for b in range(2)]
        gate_exp = m.sb("gate_exp", [P, H, TOPK])
        gate_sum = m.sb("gate_sum", [P, H])
        sel_t = m.sb("sel_t", [P, 2, P])
        gate_hi, gate_lo = m.sb("gate_hi", [P, P], F32R), m.sb("gate_lo", [P, P], F32R)
        iota, sel = R.iota, R.sel
        ident = m.sb("e_ident", [P, P])
        hot_i = [m.sb(f"hot_i{c}", [P, 8, P], F32R) for c in range(2)]
        hot_j = [m.sb(f"hot_j{c}", [P, 8, 2, P], F32R) for c in range(2)]
        parts = [m.sb(f"gate_parts{u}", [P, 2, 2, P]) for u in range(4)]
        stage = [m.sb(f"stage{f}", [P, P, 64]) for f in range(2)]
        s_ps = [m.ps(f"e_ps{b}", [P, NSEQ, L]) for b in range(2)]
        g_ps = [m.ps(f"gate_ps{b}", [P, 2, 2, P]) for b in range(2)]
        tr_ps = m.ps("tr_ps", [P, 3, P])
        const_in = m.sem("e_const_in")
        sc_in = [m.sem(f"e_sc_in{b}") for b in range(2)]
        gel_read = [m.sem(f"e_gel_read{b}") for b in range(2)]
        gel_stored = [m.sem(f"e_gel_stored{b}") for b in range(2)]
        gate_stored = [m.sem(f"e_gate_stored{f}") for f in range(2)]
        exp_done, sel_done, turned, sel_t_done, edge_steps = (m.sem(f"e_{n}") for n in (
            "exp_done", "sel_done", "turned", "sel_t_done", "edge_steps"))
        routed = R.routed
        hot_done = [m.sem(f"e_hot_done{c}") for c in range(2)]
        gates_done = m.sem("e_gates_done")
        parts_done = m.sem("e_parts_done")
        parts_summed = [m.sem(f"e_parts_summed{u}") for u in range(4)]
        block = ctx.enter_context(nc.Block())
        EDGE_STEPS = 4

        def steps_of_tile(eng, body):
            with eng.Fori(0, 2) as q:
                for e in range(2):
                    body(2 * q + e, q, 0, e)
            for h in range(4, 8):
                body(h, h // 2 % 2, 1, h % 2)

        @block.sync
        def _(sp):
            m.start_at_one(sp)
            sp.dma_start(ident[:], dram["ident"]).then_inc(const_in, 16)

            def load_scores(r, e):
                sp.wait_ge(routed, ONE + r - e)
                sp.dma_start(sc[e][:].rearrange("p h k -> p (h k)"),
                             dram["scores_flat"][bass.ds(r, 1)]).then_inc(sc_in[e], 16)

            def load_u(n):
                for b in range(2):
                    sp.wait_ge(st.lo_done, ONE + 2 * n)
                    sp.dma_start(st.raw[b][:], dram["peer_u"][bass.ds(2 * n + b, 1)]).then_inc(st.landed[b], 16)

            with sp.Fori(0, TT - 1) as tt:
                def body(h, q, half, e):
                    load_u(tt * H + h)
                    load_scores((tt + 1) * H + h, e)
                steps_of_tile(sp, body)
            steps_of_tile(sp, lambda h, q, half, e: load_u((TT - 1) * H + h))

        @block.gpsimd
        def _(pool):
            def low(i, b):
                pool.wait_ge(st.hi_done, ONE + 2 * i + b + 1)
                pool.tensor_tensor(st.lo[b][:], st.raw[b][:], f32(st.hi[b][:]), ALU.subtract).then_inc(st.lo_done, 1)

            def step(tt, h, half, final):
                n = tt * H + h
                for b in range(2):
                    if not (final and b):
                        low(n + b, 1 - b)
                    if b == 0:
                        pool.wait_ge(gate_stored[half], ONE + 16 * tt)
                    for u in range(4):
                        pool.wait_ge(parts_done, ONE + 2 + 8 * n + 4 * b + u + 1)
                        t0 = (h - 4 * half) * 16 + 8 * b + 2 * u
                        pool.tensor_tensor(stage[half][:, :, bass.ds(t0, 2)].rearrange("p j t -> p t j"),
                                           parts[u][:, :, 1], parts[u][:, :, 0], ALU.add).then_inc(parts_summed[u], 1)

            low(0, 0)
            with pool.Fori(0, TT - 1) as tt:
                steps_of_tile(pool, lambda h, q, half, e: step(tt, h, half, False))
            steps_of_tile(pool, lambda h, q, half, e: step(TT - 1, h, half, half == 1 and h == H - 1))

        @block.tensor
        def _(pe):
            def turn_selection(tt):
                pe.wait_ge(sel_done, ONE + tt + 1)
                for a in range(3):
                    t = pe.transpose(tr_ps[:, a], sel[:, a], ident[:])
                t.then_inc(turned, 1)

            def step(tt, h, edge):
                n = tt * H + h
                for b in range(2):
                    pe.wait_ge(st.lo_done, ONE + 2 * n + b + 1)
                    pe.wait_ge(gel_read[b], ONE + n)
                    for k in range(KD):
                        c = slice(k * P, (k + 1) * P)
                        for s in range(NSEQ):
                            t = slice(s * L, (s + 1) * L)
                            last = products(pe, s_ps[b][:, s], st.hi[b][:, c], st.lo[b][:, c], x_hi[:, k, t],
                                            x_lo[:, k, t], k == 0, k == KD - 1)
                        if k == KD - 1:
                            last.then_inc(st.used, 1)
                        if edge and b and k == KD - 2:
                            turn_selection(tt + 1)
                        if k % 2:
                            u = k // 2
                            pe.wait_ge(hot_done[b], ONE + n + 1)
                            pe.wait_ge(parts_done, ONE + 8 * n + 4 * b + u + 1)
                            for v in range(2):
                                g = pe.matmul(g_ps[u % 2][:, v].rearrange("p a j -> p (a j)"), hot_i[b][:, 2 * u + v],
                                              hot_j[b][:, 2 * u + v].rearrange("p a j -> p (a j)"),
                                              start=True, stop=True)
                            g.then_inc(gates_done, 1)

            pe.wait_ge(const_in, ONE + 16)
            turn_selection(0)
            with pe.Fori(0, TT - 1) as tt:
                steps_of_tile(pe, lambda h, q, half, e: step(tt, h, half == 1 and h == H - 1))
            steps_of_tile(pe, lambda h, q, half, e: step(TT - 1, h, False))

        @block.scalar
        def _(act):
            def gates_exp(tt):
                act.wait_ge(routed, ONE + (tt + 1) * H)
                act.activation(gate_exp[:], sel[:, 2].rearrange("p (h r) -> p h r", h=H), ACT.Exp).then_inc(exp_done, 1)

            def step(tt, h, half, e, edge, final):
                n = tt * H + h
                for b in range(2):
                    if edge and b:
                        gates_exp(tt + 1)
                    if not (final and b):
                        split_next(act, st, n, b)
                    for u in range(4):
                        act.wait_ge(gates_done, ONE + 8 * n + 4 * b + u + 1)
                        act.wait_ge(parts_summed[u], ONE + 2 * n + b)
                        act.activation(parts[u][:], g_ps[u % 2][:], ACT.Copy).then_inc(parts_done, 1)
                    act.wait_ge(st.used, ONE + 2 * n + b + 1)
                    act.wait_ge(gel_stored[b], ONE + 16 * n)
                    act.activation(gel[b][:], s_ps[b][:].rearrange("p s t -> p (s t)"),
                                   ACT.Gelu_apprx_tanh).then_inc(gel_read[b], 1)
                    act.wait_ge(gel_read[b], ONE + n + 1)
                    act.dma_start(dram["act"][bass.ds(2 * n + b, 1)], gel[b][:]).then_inc(gel_stored[b], 16)

            def token_tile(tt, final):
                for half in range(2):
                    if half == 0:
                        with act.Fori(0, 2) as q:
                            for e in range(2):
                                step(tt, 2 * q + e, half, e, False, False)
                    else:
                        for h in range(4, 8):
                            step(tt, h, half, h % 2, h == H - 1 and not final, h == H - 1 and final)
                    for u in range(4):
                        act.wait_ge(parts_summed[u], ONE + 16 * tt + 8 * half + 8)
                    act.dma_start(dram["gates"][bass.ds(2 * tt + half, 1)],
                                  stage[half][:].rearrange("p j t -> p (j t)")).then_inc(gate_stored[half], 16)

            act.sem_inc(parts_done, 2)
            gates_exp(0)
            split_first(act, st)
            with act.Fori(0, TT - 1) as tt:
                token_tile(tt, False)
            token_tile(TT - 1, True)
            for b in range(2):
                act.wait_ge(gel_stored[b], ONE + 16 * (P // 2))
                act.wait_ge(gate_stored[b], ONE + 16 * TT)

        @block.vector
        def _(dve):
            def build(n, h, c, done):
                dve.wait_ge(gates_done, ONE + done)
                for v in range(8):
                    t = h * 16 + 8 * c + v
                    dve.tensor_scalar(hot_i[c][:, v], iota[:], sel_t[:, 0, bass.ds(t, 1)], None, ALU.is_equal)
                    for part, gate in enumerate((gate_lo, gate_hi)):
                        last = dve.tensor_scalar(hot_j[c][:, v, part], iota[:], sel_t[:, 1, bass.ds(t, 1)],
                                                 f32(gate[:, bass.ds(t, 1)]), ALU.is_equal, ALU.mult)
                last.then_inc(hot_done[c], 1)

            def edge(tt):
                s = Steps(dve, edge_steps, tt * EDGE_STEPS, ONE)
                dve.wait_ge(exp_done, ONE + tt + 1)
                s.did(dve.tensor_reduce(gate_sum[:], gate_exp[:], X, ALU.add))
                s.settle()
                s.did(dve.reciprocal(gate_sum[:], gate_sum[:]))
                s.settle()
                dve.tensor_tensor(sel[:, 2].rearrange("p (h r) -> p h r", h=H), gate_exp[:],
                                  gate_sum[:].unsqueeze(2).broadcast_to([P, H, TOPK]), ALU.mult).then_inc(sel_done, 1)
                dve.wait_ge(turned, ONE + tt + 1)
                s.did(dve.tensor_copy(gate_hi[:], tr_ps[:, 2]))
                dve.tensor_copy(sel_t[:], tr_ps[:, 0:2]).then_inc(sel_t_done, 1)
                s.settle()
                dve.tensor_tensor(gate_lo[:], tr_ps[:, 2], f32(gate_hi[:]), ALU.subtract).then_inc(sel_t_done, 1)
                dve.wait_ge(sel_t_done, ONE + 2 * tt + 2)
                s.did(carry_wait(R, dve, 1))
                assert s.n == EDGE_STEPS

            def step(tt, h, q, half, e, routes):
                n = tt * H + h
                build(n, h, 1, 8 * n)
                if routes:
                    dve.wait_ge(sc_in[e], ONE + 16 * (tt * 4 + 2 * half + q) + 16)
                    route(R, dve, sc[e], h, (n + H) * Routing.STEPS)
                if not (half == 1 and h == H - 1):
                    build(n + 1, h + 1, 0, 8 * n + 4)
                elif routes:
                    edge(tt + 1)
                    build(n + 1, 0, 0, 8 * n + 4)

            dve.wait_ge(const_in, ONE + 16)
            edge(0)
            build(0, 0, 0, 0)
            with dve.Fori(0, TT - 1) as tt:
                steps_of_tile(dve, lambda h, q, half, e: step(tt, h, q, half, e, True))
            steps_of_tile(dve, lambda h, q, half, e: step(TT - 1, h, q, half, e, False))


def experts_out(nc, dram, out):
    GJ = 4
    NG = P // GJ
    with ExitStack() as ctx:
        m = Mem(nc, ctx)
        acc = m.sb("acc", [P, TT, D])
        a_raw = [m.sb(f"a_raw{b}", [P, T // 64, 64]) for b in range(2)]
        g_raw = [m.sb(f"g_raw{b}", [P, T // 64, 2 * 64]) for b in range(2)]
        v_raw = [m.sb(f"v_raw{b}", [P, D]) for b in range(2)]
        a_hi = [m.sb(f"a_hi{g}", [P, GJ, T], F32R) for g in range(2)]
        a_lo = [m.sb(f"a_lo{g}", [P, GJ, T], F32R) for g in range(2)]
        v_hi = [m.sb(f"v_hi{g}", [P, GJ, D], F32R) for g in range(2)]
        v_lo = [m.sb(f"v_lo{g}", [P, GJ, D], F32R) for g in range(2)]
        ps = [m.ps(f"o_ps{n}", [P, 512]) for n in range(8)]
        h_in, a_in, g_in, v_in = (m.sem("o_h_in"), [m.sem(f"o_a_in{b}") for b in range(2)],
                                  [m.sem(f"o_g_in{b}") for b in range(2)], [m.sem(f"o_v_in{b}") for b in range(2)])
        gated, ahi, alo, vhi, vlo, summed, bank_free = (m.sem(f"o_{n}") for n in (
            "gated", "ahi", "alo", "vhi", "vlo", "summed", "bank_free"))
        gain_in, squared, ms, root, inv, normed, stored = (m.sem(f"o_{n}") for n in (
            "gain_in", "squared", "ms", "root", "inv", "normed", "stored"))
        block = ctx.enter_context(nc.Block())
        JOBS = TT * 2

        @block.sync
        def _(sp):
            m.start_at_one(sp)

            def load_group(g):
                for pair in range(2):
                    i = 2 * g + pair
                    sp.wait_ge(gated, ONE + 4 * g)
                    sp.dma_start(g_raw[pair][:], dram["gates"].rearrange("b i (j t) -> i b j t", t=64)[
                        :, :, bass.ds(2 * i, 2)].rearrange("i b j t -> i b (j t)")).then_inc(g_in[pair], 16)
                    for b in range(2):
                        sp.wait_ge(alo, ONE + 2 * i)
                        sp.dma_start(a_raw[b][:].rearrange("p a t -> p (a t)"),
                                     dram["act"][bass.ds(2 * i + b, 1)]).then_inc(a_in[b], 16)
                        sp.wait_ge(vlo, ONE + 2 * i)
                        sp.dma_start(v_raw[b][:], dram["peer_v"][bass.ds(2 * i + b, 1)]).then_inc(v_in[b], 16)
            load_group(0)
            sp.dma_start(acc[:].rearrange("p n d -> p (n d)"), dram["h"]).then_inc(h_in, 16)
            with sp.Fori(1, NG) as g:
                load_group(g)
            sp.wait_ge(vlo, ONE + P)
            sp.dma_start(v_raw[0][:], dram["normf_g"].broadcast_to([P, D])).then_inc(gain_in, 16)
            for tt in range(TT):
                sp.wait_ge(normed, ONE + tt + 1)
                sp.dma_start(out[tt // LT][tt % LT * P:(tt % LT + 1) * P, :], acc[:, tt]).then_inc(stored, 16)
            sp.wait_ge(stored, ONE + 16 * TT)

        def each_group(eng, body, first=0, last=NG):
            with eng.Fori(0, (last - first) // 2) as i:
                for w in range(2):
                    body(2 * i + first + w, w)
            if (last - first) % 2:
                body(last - 1, 0)

        @block.gpsimd
        def _(pool):
            def body(g, w):
                for k in range(GJ):
                    pool.wait_ge(vhi, ONE + 4 * g + k + 1)
                    pool.tensor_tensor(v_lo[w][:, k], v_raw[k % 2][:], f32(v_hi[w][:, k]), ALU.subtract).then_inc(vlo, 1)
            each_group(pool, body)

        @block.scalar
        def _(act):
            def body(g, w):
                for k in range(GJ):
                    if k == 0:
                        act.wait_ge(summed, ONE + JOBS * (g + 1))
                    act.wait_ge(v_in[k % 2], ONE + 16 * (2 * g + k // 2) + 16)
                    act.activation(v_hi[w][:, k], v_raw[k % 2][:], ACT.Copy).then_inc(vhi, 1)
                    act.wait_ge(gated, ONE + 4 * g + k + 1)
                    act.activation(a_hi[w][:, k], a_raw[k % 2][:].rearrange("p a t -> p (a t)"), ACT.Copy).then_inc(ahi, 1)
            each_group(act, body)
            sq = g_raw[0][:].rearrange("p a t -> p (a t)")[:, 0:D]
            for tt in range(TT):
                ss = g_raw[1][:, tt, 0:1]
                act.wait_ge(bank_free, ONE + (NG - 1) * JOBS + 8 + 2 * tt + 2)
                act.wait_ge(squared, ONE + tt)
                act.activation(sq, acc[:, tt], ACT.Square, accum_out=ss).then_inc(squared, 1)
                act.wait_ge(ms, ONE + tt + 1)
                act.activation(ss, ss, ACT.Sqrt).then_inc(root, 1)

        @block.vector
        def _(dve):
            def prepare(g, w, k):
                b = k % 2
                dve.wait_ge(a_in[b], ONE + 16 * (2 * g + k // 2) + 16)
                if b == 0:
                    dve.wait_ge(g_in[k // 2], ONE + 16 * g + 16)
                dve.tensor_tensor(a_raw[b][:], a_raw[b][:], g_raw[k // 2][:, :, b * 64:(b + 1) * 64],
                                  ALU.mult).then_inc(gated, 1)
                dve.wait_ge(ahi, ONE + 4 * g + k + 1)
                dve.tensor_tensor(a_lo[w][:, k], a_raw[b][:].rearrange("p a t -> p (a t)"), f32(a_hi[w][:, k]),
                                  ALU.subtract).then_inc(alo, 1)

            def add(g, k, width=4):
                for n in range(width * k, width * k + width):
                    dve.wait_ge(summed, ONE + JOBS * (g + 2) + n + 1)
                    part = acc[:, n // 2, n % 2 * 512:(n % 2 + 1) * 512]
                    dve.tensor_tensor(part, part, ps[n % 8][:], ALU.add).then_inc(bank_free, 1)

            dve.nop().then_inc(bank_free, 8)
            for k in range(GJ):
                prepare(0, 0, k)
            dve.wait_ge(h_in, ONE + 16)

            def body(g, w):
                for k in range(GJ):
                    prepare(g + 1, 1 - w, k)
                    add(g, k)

            each_group(dve, body, 0, NG - 1)

            def mean_square(tt):
                ss = g_raw[1][:, tt, 0:1]
                dve.wait_ge(squared, ONE + tt + 1)
                dve.tensor_scalar(ss, ss, 1.0 / D, EPS, ALU.mult, ALU.add).then_inc(ms, 1)

            def normalise(tt):
                ss = g_raw[1][:, tt, 0:1]
                dve.wait_ge(root, ONE + tt + 1)
                dve.reciprocal(ss, ss).then_inc(inv, 1)
                dve.wait_ge(inv, ONE + tt + 1)
                dve.scalar_tensor_tensor(out=acc[:, tt], in0=acc[:, tt], scalar=ss, in1=v_raw[0][:],
                                         op0=ALU.mult, op1=ALU.mult).then_inc(normed, 1)

            for tt in range(TT):
                add(NG - 1, tt, 2)
                if tt:
                    mean_square(tt - 1)
                if tt == 1:
                    dve.wait_ge(gain_in, ONE + 16)
                if tt:
                    normalise(tt - 1)
            mean_square(TT - 1)
            normalise(TT - 1)

        @block.tensor
        def _(pe):
            pe.nop().then_inc(summed, 2 * JOBS)

            def body(g, w):
                pe.wait_ge(alo, ONE + 4 * g + 4)
                pe.wait_ge(vlo, ONE + 4 * g + 4)
                jobs(g, w, 0)

            def jobs(g, w, first):
                for n in range(first, JOBS):
                    tt, c = n // 2, slice(n % 2 * 512, (n % 2 + 1) * 512)
                    t = slice(tt * P, (tt + 1) * P)
                    pe.wait_ge(bank_free, ONE + JOBS * g + n + 1)
                    for k in range(GJ):
                        last = products(pe, ps[n % 8][:], a_hi[w][:, k, t], a_lo[w][:, k, t], v_hi[w][:, k, c],
                                        v_lo[w][:, k, c], k == 0, k == GJ - 1)
                    last.then_inc(summed, 1)

            def first_group():
                for k in range(GJ):
                    pe.wait_ge(alo, ONE + k + 1)
                    pe.wait_ge(vlo, ONE + k + 1)
                    for n in range(8):
                        tt, c = n // 2, slice(n % 2 * 512, (n % 2 + 1) * 512)
                        t = slice(tt * P, (tt + 1) * P)
                        if k == 0:
                            pe.wait_ge(bank_free, ONE + n + 1)
                        last = products(pe, ps[n][:], a_hi[0][:, k, t], a_lo[0][:, k, t], v_hi[0][:, k, c],
                                        v_lo[0][:, k, c], k == 0, k == GJ - 1)
                        if k == GJ - 1:
                            last.then_inc(summed, 1)
                jobs(0, 0, 8)

            first_group()
            body(1, 1)
            each_group(pe, body, 2)



def program(nc, dram, out):
    with ExitStack() as x_ctx, ExitStack() as branch_ctx:
        with ExitStack() as k_ctx:
            k = Mem(nc, k_ctx, "right")
            K = {"dft_hi": k.sb("dft_hi", [P, LT, N_FFT], F32R), "dft_lo": k.sb("dft_lo", [P, LT, N_FFT], F32R),
                 "k_re": k.sb("k_re", [P, 4, C]), "k_im": k.sb("k_im", [P, 4, C]), "k_re0": k.sb("k_re0", [P, C])}
            src_ctx = ExitStack()
            src = Mem(nc, src_ctx, "right")
            x_sb, x_in = src.sb("x_sb", [P, TT, D]), [k.sem(f"x_in{s}") for s in range(NSEQ)]
            filters(nc, dram, K, x_sb, x_in)
            x = Mem(nc, x_ctx)
            K["conv_w"], K["conv_b"] = x.sb("conv_w_sb", [P, 3, 12]), x.sb("conv_b_sb", [P, 12])
            x_hi, x_lo = x.sb("xn_hi", [P, KD, T], F32R), x.sb("xn_lo", [P, KD, T], F32R)
            norm_transpose(nc, dram, "n1", x_in, x_sb, "norm1_g", None, x_hi, x_lo)
            src_ctx.close()
            z_t = Mem(nc, x_ctx).sb("z_t", [P, CT, T])
            y_ctx = ExitStack()
            y_spec = Mem(nc, y_ctx).sb("y_spec", [P, 8, NSEQ, C])
            gate_product(nc, dram, K, x_hi, x_lo, z_t)
            forward_dft(nc, dram, K, z_t, y_spec)
        inverse_dft(nc, dram, y_spec, z_t)
        y_ctx.close()
        b = Mem(nc, branch_ctx, "right")
        br_hi, br_lo = b.sb("br_hi", [P, 8, T], F32R), b.sb("br_lo", [P, 8, T], F32R)
        branches(nc, dram, K, x_hi, x_lo, z_t, br_hi, br_lo)
        gated_mix(nc, dram, x_hi, x_lo, br_hi, br_lo)
    with ExitStack() as x_ctx:
        x = Mem(nc, x_ctx, "right")
        x_hi, x_lo = x.sb("xb_hi", [P, KD, T], F32R), x.sb("xb_lo", [P, KD, T], F32R)
        with ExitStack() as ctx:
            h = Mem(nc, ctx).sb("h_sb", [P, TT, D])
            residual(nc, dram, h)
            norm_transpose(nc, dram, "n2", None, h, "norm2_g", dram["h"], x_hi, x_lo)
        with ExitStack() as ctx:
            R = Routing(Mem(nc, ctx))
            key_scores(nc, dram, R, x_hi, x_lo)
            experts_in(nc, dram, R, x_hi, x_lo)
    experts_out(nc, dram, out)


def constants():
    f64 = np.float64
    t = np.linspace(0.0, 1.0, L, dtype=np.float32).astype(f64)
    bands = (FEMB - 1) // 2
    wpos = (2.0 * np.pi * np.arange(L) / L).astype(np.float32)
    freqs = np.linspace(1e-4, bands - 1, bands).astype(np.float32)
    ang = (freqs[:, None] * wpos[None, :]).astype(np.float32).astype(f64)
    pos = np.concatenate([t[None, :], np.cos(ang), -np.sin(ang)], axis=0)
    lo, hi = np.log(1e-2) / 1.5, np.log(1e-2) / 0.3
    decay = np.exp(-t[:, None] * np.abs(np.linspace(lo, hi, C))[None, :])
    grid = 2.0 * np.pi * (np.outer(np.arange(L), np.arange(L)) % N_FFT) / N_FFT
    fwd = np.concatenate([np.cos(grid), -np.sin(grid)], axis=1)
    fwd[:, L] = (-1.0) ** np.arange(L)
    inv = fwd.T * (2.0 / N_FFT)
    inv[0] /= 2
    inv[L] /= 2
    n = np.arange(L)
    cnt = np.stack([np.minimum(n + w // 2, L) - np.maximum(n - w // 2, 0) for w in WINDOWS])

    def tiles(a):
        return a.reshape(-1, P, a.shape[-1]).transpose(1, 0, 2)

    f = lambda a: np.ascontiguousarray(a, dtype=np.float32)
    return {"filt_pos": f(pos), "decay": f(tiles(decay)), "dft": f(tiles(fwd)), "idft": f(tiles(inv)),
            "inv_cnt": f(1.0 / cnt), "ident": f(np.eye(P)), "iota": f(np.tile(np.arange(P), (P, 1)))}


def layouts(a):
    def stationary(w):
        return w.reshape(w.shape[0] // P, P, w.shape[1] // P, P).transpose(2, 1, 0, 3)

    def cols(v):
        return v.reshape(-1, P).T

    w_out = np.concatenate([stationary(a["w_pool_out"][0]), stationary(a["w_hyena_out"][0])], axis=2)
    conv = a["conv_w"][0]
    u = a["peer_u"][0].reshape(P, NK, KD, P)
    out = {
        "x0": a["x_prompt"][0].reshape(LT, P, D).transpose(1, 0, 2), "x1": a["x_sample"][0].reshape(LT, P, D).transpose(1, 0, 2),
        "norm1_g": a["norm1_g"], "norm2_g": a["norm2_g"], "normf_g": a["normf_g"][None],
        "w_in": stationary(a["w_in"][0]).reshape(-1, P, D), "w_out": w_out.reshape(-1, P, D),
        "w_o": a["w_o"][0].reshape(KD, P, D), "wq": stationary(a["peer_wq"][0]).reshape(-1, P, D),
        "pool_w": a["pool_w"][0].transpose(1, 0, 2), "pool_scale": cols(a["pool_scale"][0]),
        "conv_w": conv.reshape(3, -1, P).transpose(2, 0, 1), "conv_b": cols(a["conv_b"][0]),
        "filt_w1": a["filt_w1"][0], "filt_w2": a["filt_w2"][0], "filt_w3": a["filt_w3"][0],
        "filt_vec": np.stack([a["filt_b1"][0], a["filt_f1"][0], a["filt_b2"][0], a["filt_f2"][0]], axis=1),
        "hyena_bias": cols(a["hyena_bias"][0]),
        "keys": a["peer_keys"][0].reshape(2 * H, NK, P).transpose(2, 0, 1),
        "peer_u": u.transpose(1, 3, 2, 0).reshape(NK, P, D),
        "peer_v": a["peer_v"][0].reshape(P, NK, D).transpose(1, 0, 2),
    }
    return {k: np.ascontiguousarray(v) for k, v in out.items()}


SCRATCH = {
    "mixed": (KD, NSEQ, P, L), "h": (P, TT * D), "scores": (TT, H, P, 2 * NK),
    "act": (NK, P, T), "gates": (T // 64, P, NK * 64),
}


def assemble(nc, arrays):
    dram = {n: nc.dram_tensor(f"in_{n}", v.shape, F32, kind="ExternalInput").ap() for n, v in arrays.items()}
    dram["x"] = (dram["x0"], dram["x1"])
    for n, shape in SCRATCH.items():
        dram[n] = nc.dram_tensor(f"tmp_{n}", shape, F32, kind="Internal").ap()
    dram["scores_flat"] = dram["scores"].rearrange("t h p k -> (t h) p k")
    out = [nc.dram_tensor(f"out_{s}", (1, L, D), F32, kind="ExternalOutput").ap().rearrange("a t d -> (a t) d")
           for s in range(NSEQ)]
    program(nc, dram, out)


def kernel(**inputs):
    import concourse.bacc as bacc
    from concourse.bass_utils import run_bass_kernel_spmd

    arrays = {**constants(), **layouts({k: np.asarray(v) for k, v in inputs.items()})}
    nc = bacc.Bacc("TRN2", target_bir_lowering=False, num_devices=1)
    assemble(nc, arrays)
    r = run_bass_kernel_spmd(nc, [{f"in_{n}": v for n, v in arrays.items()}], core_ids=[0])
    return tuple(r.results[0][f"out_{s}"] for s in range(NSEQ))
```
